# Optimizing a Trainium2 kernel written in Bass

```python
import jax, jax.numpy as jnp
from jax import lax
import numpy as np

D_MODEL = 1024
BATCH = 1
SEQ = 1024
DEPTH = 2
DEC_BATCH = 1
DEC_SEQ = 64
PAST_LEN = 512

CHUNK = 64
Q_BLOCK = 128
EPS = 1e-6
NEG_INF = -1e30
ROPE_THETA = 10000.0
MLA_HEADS = 8
MLA_NOPE = 64
MLA_ROPE = 32
MLA_V = 64
MLA_Q_RANK = 256
MLA_KV_RANK = 256
MLA_WIDTH = MLA_HEADS * MLA_V
MLA_SCALE = (MLA_NOPE + MLA_ROPE) ** -0.5
HG_HEADS = 4
HG_DK = 64
HG_DV = 64
HG_WIDTH = HG_HEADS * HG_DV
GLA_HEADS = 4
GLA_DK = 32
GLA_DV = 64
GLA_RANK = 16
GLA_TAU = 16.0
GLA_WIDTH = GLA_HEADS * GLA_DV
MIX_WIDTH = MLA_WIDTH + HG_WIDTH + GLA_WIDTH
IN_SIZES = (MLA_Q_RANK, MLA_KV_RANK, MLA_ROPE,
            HG_HEADS * HG_DK, HG_HEADS * HG_DK, HG_WIDTH, HG_WIDTH,
            GLA_HEADS * GLA_DK, GLA_HEADS * GLA_DK, GLA_WIDTH, GLA_WIDTH, GLA_RANK)
IN_COLS = sum(IN_SIZES)
D_FF = -(-8 * D_MODEL // (3 * 256)) * 256

kernel_name = 'hymba_mla_hgrn2_gla_stream'

def rmsnorm(x, g):
    xf = x.astype(jnp.float32)
    y = xf * lax.rsqrt(jnp.mean(xf * xf, axis=-1, keepdims=True) + EPS)
    return (y * g.astype(jnp.float32)).astype(x.dtype)

def split_projection(z):
    idx = [int(v) for v in np.cumsum(IN_SIZES)[:-1]]
    return jnp.split(z, idx, axis=-1)

def rope_angles(pos):
    inv = ROPE_THETA ** (-(jnp.arange(0, MLA_ROPE, 2, dtype=jnp.float32) / MLA_ROPE))
    ang = pos.astype(jnp.float32)[:, None] * inv[None, :]
    return jnp.cos(ang), jnp.sin(ang)

def apply_rope(x, cos, sin):
    xf = x.astype(jnp.float32)
    half = xf.shape[-1] // 2
    x1, x2 = xf[..., :half], xf[..., half:]
    return jnp.concatenate([x1 * cos - x2 * sin, x2 * cos + x1 * sin], axis=-1).astype(x.dtype)

def chunk_recurrence(q, k, v, log_f, s0):
    B, T, H, _ = q.shape
    dv = v.shape[-1]
    c = min(CHUNK, T)
    n = T // c

    def to_chunks(a):
        return jnp.moveaxis(a.astype(jnp.float32).reshape(B, n, c, H, a.shape[-1]), 1, 0)

    tril = jnp.tril(jnp.ones((c, c), dtype=bool))

    def step(S, xs):
        qc, kc, vc, gc = xs
        b = jnp.cumsum(gc, axis=1)
        o_inter = jnp.einsum('bchk,bhkv->bchv', qc * jnp.exp(b), S)
        diff = b[:, :, None] - b[:, None, :]
        decay = jnp.exp(jnp.where(tril[None, :, :, None, None], diff, -jnp.inf))
        scores = jnp.sum(qc[:, :, None] * kc[:, None] * decay, axis=-1)
        o_intra = jnp.einsum('bijh,bjhv->bihv', scores, vc)
        b_last = b[:, -1]
        S = jnp.exp(b_last)[..., None] * S + jnp.einsum(
            'bjhk,bjhv->bhkv', kc * jnp.exp(b_last[:, None] - b), vc)
        return S, o_inter + o_intra

    S, o = lax.scan(step, s0.astype(jnp.float32),
                    (to_chunks(q), to_chunks(k), to_chunks(v), to_chunks(log_f)))
    o = jnp.moveaxis(o, 0, 1).reshape(B, T, H, dv)
    return o.astype(v.dtype), S.astype(s0.dtype)

def mla_block(q_nope, q_rope, q_pos, k_nope, k_rope, ckv, k_pos, w_uv):
    s = (jnp.einsum('bqhd,bkhd->bhqk', q_nope, k_nope)
         + jnp.einsum('bqhd,bkd->bhqk', q_rope, k_rope)).astype(jnp.float32) * MLA_SCALE
    visible = (k_pos // CHUNK)[None, :] <= (q_pos // CHUNK)[:, None]
    s = jnp.where(visible[None, None], s, NEG_INF)
    p = jax.nn.softmax(s, axis=-1).astype(ckv.dtype)
    o_lat = jnp.einsum('bhqk,bkr->bqhr', p, ckv)
    return jnp.einsum('bqhr,rhd->bqhd', o_lat, w_uv)

def mla_attention(q_nope, q_rope, pos, k_nope, k_rope, ckv, k_pos, w_uv):
    B, T = q_nope.shape[:2]
    qb = min(Q_BLOCK, T)
    nb = T // qb

    def blocks(a):
        return jnp.moveaxis(a.reshape((B, nb, qb) + a.shape[2:]), 1, 0)

    out = lax.map(lambda xs: mla_block(xs[0], xs[1], xs[2], k_nope, k_rope, ckv, k_pos, w_uv),
                  (blocks(q_nope), blocks(q_rope), pos.reshape(nb, qb)))
    return jnp.moveaxis(out, 0, 1).reshape(B, T, MLA_WIDTH)

def trunk_layer(x, c, pos, ckv_past, krope_past, s_hg, s_gla, lp):
    B, T, _ = x.shape
    P = ckv_past.shape[1]
    mod = jax.nn.silu(c) @ lp['w_mod'] + lp['b_mod']
    sh1, sc1, g1, sh2, sc2, g2 = jnp.split(mod[:, None, :], 6, axis=-1)
    h = rmsnorm(x, lp['norm_mix']) * (1.0 + sc1) + sh1
    cq, ckv, kr, hq, hf, hi, hg, gq, gk, gv, gg, ga = split_projection(h @ lp['w_in'])

    cq = rmsnorm(cq, lp['mla_cq_norm'])
    ckv = rmsnorm(ckv, lp['mla_ckv_norm'])
    q = jnp.einsum('btr,rhd->bthd', cq, lp['mla_w_uq'])
    cos, sin = rope_angles(pos)
    q_nope = rmsnorm(q[..., :MLA_NOPE], lp['mla_q_norm'][:MLA_NOPE])
    q_rope = apply_rope(rmsnorm(q[..., MLA_NOPE:], lp['mla_q_norm'][MLA_NOPE:]), cos[:, None], sin[:, None])
    k_rope = apply_rope(rmsnorm(kr, lp['mla_k_norm'][MLA_NOPE:]), cos, sin)
    ckv_all = jnp.concatenate([ckv_past, ckv], axis=1)
    krope_all = jnp.concatenate([krope_past, k_rope], axis=1)
    k_pos = jnp.concatenate([jnp.arange(P, dtype=jnp.int32), pos])
    k_nope = rmsnorm(jnp.einsum('bsr,rhd->bshd', ckv_all, lp['mla_w_uk']), lp['mla_k_norm'][:MLA_NOPE])
    o_mla = rmsnorm(mla_attention(q_nope, q_rope, pos, k_nope, krope_all, ckv_all, k_pos, lp['mla_w_uv']),
                    lp['mla_out_norm'])

    lb = lp['hg_lb'].reshape(HG_HEADS, HG_DK)
    f = lb + (1.0 - lb) * jax.nn.sigmoid(hf.reshape(B, T, HG_HEADS, HG_DK).astype(jnp.float32))
    o_hg, s_hg_new = chunk_recurrence(hq.reshape(B, T, HG_HEADS, HG_DK), 1.0 - f,
                                      hi.reshape(B, T, HG_HEADS, HG_DV), jnp.log(f), s_hg)
    o_hg = rmsnorm(o_hg, lp['hg_out_norm']).reshape(B, T, HG_WIDTH) * jax.nn.silu(hg)

    log_a = jax.nn.log_sigmoid((ga @ lp['gla_w_a2'] + lp['gla_b_a']).astype(jnp.float32)) / GLA_TAU
    o_gla, s_gla_new = chunk_recurrence(gq.reshape(B, T, GLA_HEADS, GLA_DK) * GLA_DK ** -0.5,
                                        gk.reshape(B, T, GLA_HEADS, GLA_DK),
                                        gv.reshape(B, T, GLA_HEADS, GLA_DV),
                                        log_a.reshape(B, T, GLA_HEADS, GLA_DK), s_gla)
    o_gla = rmsnorm(o_gla, lp['gla_out_norm']).reshape(B, T, GLA_WIDTH) * jax.nn.silu(gg)

    mix = jnp.concatenate([o_mla, o_hg, o_gla], axis=-1) @ lp['w_o']
    x = x + g1 * mix

    h2 = rmsnorm(x, lp['norm_ffn']) * (1.0 + sc2) + sh2
    a, u = jnp.split(h2 @ lp['w_ffn_in'], 2, axis=-1)
    x = x + g2 * ((jax.nn.silu(a) * u) @ lp['w_ffn_out'])
    return x, ckv, k_rope, s_hg_new, s_gla_new

def setup_inputs(seed: int = 0) -> dict:
    key = jax.random.key(seed)
    ks = jax.random.split(key, 32)

    def nrm(k, shape, scale):
        return jax.random.normal(k, shape, jnp.float32) * scale

    def gain(k, shape):
        return 1.0 + 0.02 * jax.random.normal(k, shape, jnp.float32)

    return {
        'x_prompt': nrm(ks[0], (BATCH, SEQ, D_MODEL), 1.0),
        'x_sample': nrm(ks[1], (DEC_BATCH, DEC_SEQ, D_MODEL), 1.0),
        'c_prompt': nrm(ks[2], (BATCH, D_MODEL), 1.0),
        'c_sample': nrm(ks[3], (DEC_BATCH, D_MODEL), 1.0),
        'cache_mla_ckv': nrm(ks[4], (DEPTH, DEC_BATCH, PAST_LEN, MLA_KV_RANK), 1.0),
        'cache_mla_krope': nrm(ks[5], (DEPTH, DEC_BATCH, PAST_LEN, MLA_ROPE), 1.0),
        'state_hgrn': nrm(ks[6], (DEPTH, DEC_BATCH, HG_HEADS, HG_DK, HG_DV), 0.5),
        'state_gla': nrm(ks[7], (DEPTH, DEC_BATCH, GLA_HEADS, GLA_DK, GLA_DV), 0.5),
        'w_mod': nrm(ks[8], (DEPTH, D_MODEL, 6 * D_MODEL), D_MODEL ** -0.5),
        'b_mod': nrm(ks[9], (DEPTH, 6 * D_MODEL), 0.02),
        'norm_mix': gain(ks[10], (DEPTH, D_MODEL)),
        'norm_ffn': gain(ks[11], (DEPTH, D_MODEL)),
        'w_in': nrm(ks[12], (DEPTH, D_MODEL, IN_COLS), D_MODEL ** -0.5),
        'mla_cq_norm': gain(ks[13], (DEPTH, MLA_Q_RANK)),
        'mla_ckv_norm': gain(ks[14], (DEPTH, MLA_KV_RANK)),
        'mla_w_uq': nrm(ks[15], (DEPTH, MLA_Q_RANK, MLA_HEADS, MLA_NOPE + MLA_ROPE), MLA_Q_RANK ** -0.5),
        'mla_w_uk': nrm(ks[16], (DEPTH, MLA_KV_RANK, MLA_HEADS, MLA_NOPE), MLA_KV_RANK ** -0.5),
        'mla_w_uv': nrm(ks[17], (DEPTH, MLA_KV_RANK, MLA_HEADS, MLA_V), MLA_KV_RANK ** -0.5),
        'mla_q_norm': gain(ks[18], (DEPTH, MLA_NOPE + MLA_ROPE)),
        'mla_k_norm': gain(ks[19], (DEPTH, MLA_NOPE + MLA_ROPE)),
        'mla_out_norm': gain(ks[20], (DEPTH, MLA_WIDTH)),
        'hg_lb_logits': nrm(ks[21], (DEPTH, HG_HEADS * HG_DK), 0.5),
        'hg_out_norm': gain(ks[22], (DEPTH, HG_DV)),
        'gla_w_a2': nrm(ks[23], (DEPTH, GLA_RANK, GLA_HEADS * GLA_DK), GLA_RANK ** -0.5),
        'gla_b_a': nrm(ks[24], (DEPTH, GLA_HEADS * GLA_DK), 0.1),
        'gla_out_norm': gain(ks[25], (DEPTH, GLA_DV)),
        'w_o': nrm(ks[26], (DEPTH, MIX_WIDTH, D_MODEL), MIX_WIDTH ** -0.5),
        'w_ffn_in': nrm(ks[27], (DEPTH, D_MODEL, 2 * D_FF), D_MODEL ** -0.5),
        'w_ffn_out': nrm(ks[28], (DEPTH, D_FF, D_MODEL), D_FF ** -0.5),
    }

def reference(x_prompt, x_sample, c_prompt, c_sample, cache_mla_ckv, cache_mla_krope, state_hgrn, state_gla,
              w_mod, b_mod, norm_mix, norm_ffn, w_in, mla_cq_norm, mla_ckv_norm, mla_w_uq, mla_w_uk, mla_w_uv,
              mla_q_norm, mla_k_norm, mla_out_norm, hg_lb_logits, hg_out_norm, gla_w_a2, gla_b_a, gla_out_norm,
              w_o, w_ffn_in, w_ffn_out):
    Bp, T_p = x_prompt.shape[:2]
    T_s = x_sample.shape[1]
    pos_p = jnp.arange(T_p, dtype=jnp.int32)
    pos_s = PAST_LEN + jnp.arange(T_s, dtype=jnp.int32)
    p_lb = jax.nn.softmax(hg_lb_logits.astype(jnp.float32), axis=0)
    lb_all = jnp.cumsum(p_lb, axis=0) - p_lb[0:1]

    dt = x_prompt.dtype
    ckv0 = jnp.zeros((Bp, 0, MLA_KV_RANK), dt)
    kr0 = jnp.zeros((Bp, 0, MLA_ROPE), dt)
    shg0 = jnp.zeros((Bp, HG_HEADS, HG_DK, HG_DV), dt)
    sgla0 = jnp.zeros((Bp, GLA_HEADS, GLA_DK, GLA_DV), dt)

    xp, xs = x_prompt, x_sample
    ckv_p, kr_p, hg_p, gla_p = [], [], [], []
    ckv_s, kr_s, hg_s, gla_s = [], [], [], []
    for l in range(DEPTH):
        lp = {'w_mod': w_mod[l], 'b_mod': b_mod[l], 'norm_mix': norm_mix[l], 'norm_ffn': norm_ffn[l],
              'w_in': w_in[l], 'mla_cq_norm': mla_cq_norm[l], 'mla_ckv_norm': mla_ckv_norm[l],
              'mla_w_uq': mla_w_uq[l], 'mla_w_uk': mla_w_uk[l], 'mla_w_uv': mla_w_uv[l],
              'mla_q_norm': mla_q_norm[l], 'mla_k_norm': mla_k_norm[l], 'mla_out_norm': mla_out_norm[l],
              'hg_lb': lb_all[l], 'hg_out_norm': hg_out_norm[l], 'gla_w_a2': gla_w_a2[l],
              'gla_b_a': gla_b_a[l], 'gla_out_norm': gla_out_norm[l], 'w_o': w_o[l],
              'w_ffn_in': w_ffn_in[l], 'w_ffn_out': w_ffn_out[l]}
        xp, a, b, cc, d = trunk_layer(xp, c_prompt, pos_p, ckv0, kr0, shg0, sgla0, lp)
        ckv_p.append(a); kr_p.append(b); hg_p.append(cc); gla_p.append(d)
        xs, a, b, cc, d = trunk_layer(xs, c_sample, pos_s, cache_mla_ckv[l], cache_mla_krope[l],
                                      state_hgrn[l], state_gla[l], lp)
        ckv_s.append(a); kr_s.append(b); hg_s.append(cc); gla_s.append(d)

    new_ckv_prompt = jnp.stack(ckv_p)
    new_krope_prompt = jnp.stack(kr_p)
    new_hgrn_prompt = jnp.stack(hg_p)
    new_gla_prompt = jnp.stack(gla_p)
    new_ckv_sample = jnp.stack(ckv_s)
    new_krope_sample = jnp.stack(kr_s)
    new_hgrn_sample = jnp.stack(hg_s)
    new_gla_sample = jnp.stack(gla_s)
    return (xp, xs, new_ckv_prompt, new_krope_prompt, new_hgrn_prompt, new_gla_prompt,
            new_ckv_sample, new_krope_sample, new_hgrn_sample, new_gla_sample)


_drawn_inputs = setup_inputs


def setup_inputs(seed=0):
    import zlib

    import numpy as np

    out = dict(_drawn_inputs(seed))
    spreads = {}
    factors = {'norm_mix': 2.889,
     'norm_ffn': 2.966,
     'mla_cq_norm': 6.297,
     'mla_ckv_norm': 2.875,
     'mla_q_norm': 6.746,
     'mla_k_norm': 2.818,
     'mla_out_norm': 25.549,
     'hg_out_norm': 8.0,
     'gla_out_norm': 8.0,
     'state_gla': 2.809}
    for name, (base, spread) in spreads.items():
        noise = np.random.default_rng([zlib.crc32(name.encode()), seed]).standard_normal(out[name].shape)
        drawn = base * np.exp(spread * noise) if base else spread * noise
        out[name] = __import__('jax').numpy.asarray(drawn.astype(out[name].dtype))
    for name, factor in factors.items():
        out[name] = (out[name] * factor).astype(out[name].dtype)
    return out
```

```python
import contextlib

import numpy as np

import concourse.bass as bass
from concourse import mybir

F32 = mybir.dt.float32
F32R = mybir.dt.float32r
I32 = mybir.dt.int32
ALU = mybir.AluOpType
ACT = mybir.ActivationFunctionType
AX = mybir.AxisListType

P = 128
D_MODEL, SEQ, DEC_SEQ, PAST, DEPTH = 1024, 1024, 64, 512, 2
TOK = SEQ + DEC_SEQ
CHUNK = 64
EPS = 1e-6
KT8 = D_MODEL // P
CHUNKS = [(0, 384), (384, 384), (768, 320)]
TILES = [(P * t, P) for t in range(SEQ // P)] + [(SEQ, DEC_SEQ)]
NTILE = len(TILES)
HEADS, NOPE, ROPE, VDIM, RANK = 8, 64, 32, 64, 256
QK = NOPE + ROPE
MLA_SCALE = QK ** -0.5
MLA_W = HEADS * VDIM
HG_H, GLA_H, HG_DK, GLA_DK, DV = 4, 4, 64, 32, 64
GLA_SCALE = GLA_DK ** -0.5
TAU = 16.0
F_MIN = 1e-19
D_FF = 2816
GROUP = 256
NGROUP = D_FF // GROUP
C_CQ, C_CKV, C_KR, C_HQ, C_HF, C_HI, C_HG, C_GQ, C_GK, C_GV, C_GG, C_GA, IN_COLS = (
    0, 256, 512, 544, 800, 1056, 1312, 1568, 1696, 1824, 2080, 2336, 2352)
FM_COLS = [C_HQ, C_HF, C_GQ]
TM_COLS = [C_CQ, C_CKV, C_HI, C_HG, C_GV, C_GG]
ZT_W = 6 * 256 + 48
ZT_KR, ZT_GA = 1536, 1568
SLOT = 2048
NMOD = 24
MASK_NEG = -1e30

O_ID, O_ONES, O_COS, O_SIN, O_EPS, O_MQ, O_MK, CST_W = 0, 128, 256, 400, 544, 576, 704, 832
R_RM, R_BM, R_LM, CSTR_W = 0, 128, 640, 640 + 6 * 128
LEVELS = [1, 2, 4, 8, 16, 32]


def constants():
    c = np.zeros((P, CST_W), np.float32)
    c[:, O_ID:O_ID + P] = np.eye(P)
    c[:, O_ONES:O_ONES + P] = 1.0 / D_MODEL
    inv = np.float32(10000.0) ** (-(np.arange(0, ROPE, 2, dtype=np.float32) / np.float32(ROPE)))
    for t, (t0, n) in enumerate(TILES):
        pos = np.arange(n, dtype=np.float32) + (t0 if t < NTILE - 1 else PAST)
        ang = (pos[:, None] * inv[None, :]).astype(np.float32)
        c[:n, O_COS + 16 * t:O_COS + 16 * t + 16] = np.cos(ang)
        c[:n, O_SIN + 16 * t:O_SIN + 16 * t + 16] = np.sin(ang)
    c[:, O_EPS] = EPS
    c[0, O_MQ:O_MQ + CHUNK] = MASK_NEG
    c[0, O_MK + CHUNK:O_MK + P] = 1.0
    r = np.zeros((P, CSTR_W), np.float32)
    r[:, R_RM:R_RM + P] = 1.0
    r[:, R_RM] = 0.0
    r[:, R_RM + CHUNK] = 0.0
    bm = np.zeros((P, 8, DV), np.float32)
    for h in range(HG_H):
        bm[64 * (h % 2):64 * (h % 2) + 64, h] = 1.0
    for h in range(GLA_H):
        bm[32 * h:32 * h + 32, 4 + h] = 1.0
    r[:, R_BM:R_BM + 512] = bm.reshape(P, 512)
    j, i = np.meshgrid(np.arange(P), np.arange(P), indexing="ij")
    for n, b in enumerate(LEVELS):
        m = (j // (2 * b) == i // (2 * b)) & (j % (2 * b) < b) & (i % (2 * b) >= b)
        r[:, R_LM + P * n:R_LM + P * n + P] = m
    return c, r


AHEAD = ("ffn_pe", "ffn_dve", "r_dve")


class Steps:

    def __init__(self, sem, plan, name):
        self.sem, self.name = sem, name
        self.known = plan.get(name)
        self.seen = []
        self.bodies = 0

    @property
    def length(self):
        return len(self.known) if self.known else 1

    def value(self, turn, step):
        at = self.known.index(step) + 1 if self.known else 1
        return (turn + (2 if self.name in AHEAD else 0)) * self.length + at

    def done(self, ins, step):
        if self.bodies == 0:
            assert step not in self.seen, (self.name, step)
            self.seen.append(step)
        else:
            assert self.seen[self.at] == step, (self.name, step, self.seen[self.at])
            self.at += 1
        ins.then_inc(self.sem, 1)

    def body(self):
        if self.seen:
            self.bodies += 1
            self.at = 0


def program(nc, io, plan):
    ctx = contextlib.ExitStack()
    steps = {}

    def sem(name):
        return ctx.enter_context(nc.semaphore(name))

    def st(name):
        if name not in steps:
            steps[name] = Steps(sem("s_" + name), plan, name)
        return steps[name]

    zf_d = nc.dram_tensor("z_feature_major", [6, P, TOK], F32, kind="Internal").ap()
    zt_d = nc.dram_tensor("z_token_major", [TOK, ZT_W], F32, kind="Internal").ap()
    mix_d = nc.dram_tensor("mixer_out", [TOK, D_MODEL], F32, kind="Internal").ap()

    top = [16512]

    def place(name, shape, dt, at=None):
        size = int(np.prod(shape[1:])) * 4
        off = top[0] if at is None else at[0]
        t = nc.alloc_sbuf_tensor_at(name, shape, dt, offset=off)
        if at is None:
            top[0] = off + (size + 31) // 32 * 32
        else:
            at[0] = off + (size + 31) // 32 * 32
            assert at[0] <= at[1], (name, at)
        return t

    X = place("x", [P, KT8, TOK], F32)
    a_at = top[0]
    A = place("act_split", [P, 2, KT8, TOK], F32R)
    a_end = top[0]
    W = place("w_split", [P, 3, 2, SLOT], F32R)
    WR = place("w_raw", [P, 3, SLOT], F32)
    h_at = top[0]
    HID = place("hidden_split", [P, 2, 2, TOK], F32R)
    h_end = top[0]
    MR = place("w_mod_raw", [P, 2, SLOT], F32, [h_at, h_end])
    CST = place("cst", [P, CST_W], F32)
    KGS = place("w_krga_split", [P, 2, KT8, 48], F32R)
    PRR = place("param_rows", [P, P], F32)
    PRM = place("param_cols", [P, 65], F32)
    MOD = place("mod", [P, 48, 2], F32)
    GS = place("gain_scale", [P, KT8, 2], F32)
    SCV = place("silu_c", [P, KT8, 2], F32)
    LB = place("lower_bound", [P, 2 * DEPTH], F32)
    LBL = place("lower_bound_layer", [P, 4], F32)
    WA2 = place("w_a2", [16, P], F32)
    SM = place("small_setup", [P, 64], F32)
    lt_at, lt_end = top[0], 229344
    a = [lt_at, lt_end]
    SQ = place("norm_sq", [P, 2, 384], F32, a)
    TN = place("norm_t", [P, 2, 384], F32, a)
    RS = place("norm_rs", [P, 384], F32, a)
    a = [lt_at, lt_end]
    ZS = place("z_stage", [P, 3, 384], F32, a)
    a = [lt_at, lt_end]
    SIL = place("silu_a", [P, 2, 384], F32, a)
    HF32 = place("hidden_f32", [P, 2, 384], F32, a)
    KGW = place("w_krga_raw", [P, KT8, 48], F32, [a_at, a_end])
    a = [a_at, a_end]
    XT = place("x_token_major", [P, 2, D_MODEL], F32, a)
    a = [h_at, h_end]
    MT = place("mix_token_major", [P, 2, D_MODEL], F32, a)

    a = [a_at, a_end]
    r_cst = place("r_cst", [P, CSTR_W], F32, a)
    rQQ = place("r_q", [P, 2, 3, P], F32, a)
    rKK = place("r_k", [P, 2, 3, P], F32, a)
    rHF = place("r_hf", [P, 2, 2, P], F32, a)
    rV = place("r_v", [P, 2, 2, 512], F32, a)
    rGA = place("r_ga", [P, 2, 16], F32, a)
    rT1 = place("r_sigma", [P, 2, P], F32, a)
    rT2 = place("r_abs", [P, P], F32, a)
    rT3 = place("r_neg", [P, P], F32, a)
    rG = place("r_logf", [P, 3, P], F32, a)
    rB = place("r_b", [P, 3, P], F32, a)
    rD = place("r_d", [P, 2, 3, P], F32, a)
    rE = place("r_e", [P, 2, 3, P], F32, a)
    rKE = place("r_ke", [P, 2, 3, P], F32, a)
    rQX = place("r_qx", [P, 2, 8, P], F32, a)
    rP = place("r_p", [P, 8, P], F32, a)
    rKT = place("r_kt", [P, 3, P], F32, a)
    rS = place("r_state", [P, 2, 512], F32, a)
    rDS = place("r_ds", [P, 512], F32, a)
    rO = place("r_o", [P, 512], F32, a)
    rON = place("r_on", [P, 512], F32, a)
    rEG = place("r_eg", [P, 512], F32, a)
    rOUT = place("r_out", [P, 2, 512], F32, a)
    rGT = place("r_gat", [16, P], F32, a)
    rGN = place("r_gain", [P, 2, DV], F32, a)
    rSS = place("r_ss", [P, 8], F32, a)

    a = [a_at, a_end]
    KTt = place("k_t", [QK, HEADS, SEQ], F32, a)
    Vt = place("v_tm", [P, 8, 512], F32, a)
    GN = place("mla_gains", [P, 256 + 256 + QK + QK + 512], F32, a)
    QT = place("q_t", [QK, HEADS, P], F32, a)
    ZT = place("z_tile", [P, 544], F32, a)
    CT = place("c_t", [P, 4, P], F32, a)
    KM = place("k_tm", [P, HEADS, QK], F32, a)
    QM = place("q_tm", [P, HEADS, QK], F32, a)
    a = [h_at, h_end]
    PB = place("probs", [P, 2, SEQ], F32, a)
    PT = place("probs_t", [P, 2, 8, P], F32, a)
    a = [lt_at, lt_end]
    QSQ = place("qk_sq", [P, 768], F32, a)
    ROT = place("rot", [P, HEADS, ROPE], F32, a)
    OM = place("o_mla", [P, 512], F32, a)
    AS = place("a_stats", [P, 64], F32, a)

    ps = [ctx.enter_context(nc.psum_tensor(f"bank{i}", [P, 512], F32)) for i in range(8)]

    raw_ld = [sem(f"raw_loaded{r}") for r in range(3)]
    RAW_N = 49
    SPLIT_N = 46
    raw_cnt = [len(range(r, RAW_N, 3)) for r in range(3)]
    w_hi, w_lo = sem("w_hi_done"), sem("w_lo_done")
    mod_ld = [sem("mod_loaded0"), sem("mod_loaded1")]
    mod_pe, mod_dve = sem("mod_summed"), sem("mod_kept")
    setup_ld = sem("setup_loaded")
    par_ld = sem("params_loaded")
    x_ld = [sem("x_loaded0"), sem("x_loaded1")]
    spill = [sem(f"z_spilled{i}") for i in range(3)]
    SPILL_N = [27, 27, 27]
    r_ld = [sem("r_tile_loaded0"), sem("r_tile_loaded1")]
    rc_ld = sem("r_consts_loaded")
    rs_ld = sem("r_state_loaded")
    r_out = [sem("r_out_stored0"), sem("r_out_stored1")]
    rs_out = sem("r_state_stored")
    a_ld = sem("a_tile_loaded")
    ac_ld = sem("a_consts_loaded")
    a_out = sem("a_out_stored")
    kv_out = sem("kv_stored")
    m_ld = [sem("mix_loaded0"), sem("mix_loaded1")]
    y_out = [sem("y_stored0"), sem("y_stored1")]

    def raw_ready(l, n):
        return (l * raw_cnt[n % 3] + n // 3 + 1) * 16

    def hi_val(l, m):
        return l * SPLIT_N + m + 1

    def lo_val(l, m):
        return l * SPLIT_N + m + 2

    waited = sem("waited")

    def settle(eng):
        eng.sem_inc(waited, 1)

    def wait(eng, name, turn, step):
        s = st(name)
        eng.wait_ge(s.sem, s.value(turn, step))

    def prime(eng, *names):
        for n in names:
            assert n in AHEAD
            eng.sem_inc(st(n).sem, 2 * st(n).length)

    w_in_v = io["w_in"].rearrange("l (k p) c -> l p k c", p=P)
    w_mod_v = io["w_mod"].rearrange("l (k p) c -> l p k c", p=P)
    w_o_v = io["w_o"].rearrange("l (k p) c -> l p k c", p=P)
    w_f1_v = io["w_ffn_in"].rearrange("l (k p) c -> l p k c", p=P)
    w_f2_v = io["w_ffn_out"].rearrange("l (k p) c -> l p k c", p=P)
    uq_v = io["mla_w_uq"].rearrange("l (k p) h d -> l p k (h d)", p=P)
    uk_v = io["mla_w_uk"].rearrange("l (k p) h d -> l p k (h d)", p=P)
    uv_v = io["mla_w_uv"].rearrange("l (k p) h d -> l p k (h d)", p=P)
    w8 = [WR[:, r, :].rearrange("p (k c) -> p k c", k=8) for r in range(3)]
    WQ = WR[:, 0, 0:1536].rearrange("p (k c) -> p k c", k=2)
    WK = WR[:, 1, 0:1024].rearrange("p (k c) -> p k c", k=2)
    WV = WR[:, 2, 0:1024].rearrange("p (k c) -> p k c", k=2)
    xp, xs = io["x_prompt"][0], io["x_sample"][0]
    yp, ys = io["y_prompt"][0], io["y_sample"][0]
    ident = CST[:, O_ID:O_ID + P]
    EPSC = CST[:, O_EPS:O_EPS + 1]

    def rows(dram_p, dram_s, t):
        t0, n = TILES[t]
        return dram_p[t0:t0 + n] if t < NTILE - 1 else dram_s[0:n]

    with ctx:
        block = ctx.enter_context(nc.Block())

        def store_state(sp, l, hg, gla, buf):
            for h in range(HG_H):
                sp.dma_start(hg[l][0, h], rS[64 * (h % 2):64 * (h % 2) + 64, buf, 64 * h:64 * h + 64]).then_inc(rs_out, 16)
            for h in range(GLA_H):
                sp.dma_start(gla[l][0, h], rS[32 * h:32 * h + 32, buf, 256 + 64 * h:320 + 64 * h]).then_inc(rs_out, 16)

        @block.sync
        def _(sp):
            sp.dma_start(CST[:], io["cst"]).then_inc(setup_ld, 16)
            sp.dma_start(PRR[0:8, :], io["c_prompt"].rearrange("a (k p) -> (a k) p", p=P)).then_inc(setup_ld, 16)
            sp.dma_start(PRR[8:16, :], io["c_sample"].rearrange("a (k p) -> (a k) p", p=P)).then_inc(setup_ld, 16)
            sp.dma_start(PRR[16:20, :], io["hg_lb_logits"].rearrange("l (k p) -> (l k) p", p=P)).then_inc(setup_ld, 16)
            for t, (t0, n) in enumerate(TILES):
                if t >= 2:
                    wait(sp, "in_pe", 0, f"x{t - 2}b")
                sp.dma_start(XT[0:n, t % 2], rows(xp, xs, t)).then_inc(x_ld[t % 2], 16)

            def load_raw(l, n, src, k):
                r = n % 3
                dst = WR[:, r, 0:k * src.shape[-1]].rearrange("p (k c) -> p k c", k=k)
                sp.dma_start(dst, src).then_inc(raw_ld[r], 16)

            def load_mod(l, s):
                sp.dma_start(MR[:, s % 2].rearrange("p (k c) -> p k c", k=8),
                             w_mod_v[l][:, :, 256 * s:256 * s + 256]).then_inc(mod_ld[s % 2], 16)

            with sp.Fori(0, DEPTH) as l:
                sp.wait_ge(w_lo, l * SPLIT_N + 1)
                wl = w_in_v[l]
                for n in range(3):
                    load_raw(l, n, wl[:, :, FM_COLS[n]:FM_COLS[n] + 256], 8)
                wait(sp, "ffn_pe", l * NGROUP - 1, "x23")
                for s in range(8):
                    if s >= 2:
                        sp.wait_ge(mod_pe, l * NMOD + s - 1)
                    load_mod(l, s)

                order = [("w", 3), ("w", 4), ("w", 5), ("m", 8), ("m", 9), ("m", 10), ("m", 11), ("w", 6), ("m", 12),
                         ("m", 13), ("w", 7), ("m", 14), ("m", 15), ("w", 8), ("m", 16), ("m", 17), ("w", 9),
                         ("m", 18), ("m", 19), ("w", 10), ("m", 20), ("m", 21), ("w", 11), ("m", 22), ("m", 23)]
                for kind, n in order:
                    if kind == "m":
                        sp.wait_ge(mod_pe, l * NMOD + n - 1)
                        load_mod(l, n)
                    else:
                        sp.wait_ge(w_lo, lo_val(l, n - 3))
                        if n < 9:
                            c = TM_COLS[n - 3]
                            load_raw(l, n, wl[:, :, c:c + 256], 8)
                        else:
                            load_raw(l, n, [uq_v, uk_v, uv_v][n - 9][l], 2)

                for i in range(3):
                    sp.wait_ge(spill[i], (l + 1) * SPILL_N[i] * 16)
                sp.dma_start(r_cst[:], io["cst_r"]).then_inc(rc_ld, 16)
                sp.dma_start(rGN[:, 0], io["hg_out_norm"][l].unsqueeze(0).broadcast_to([P, DV])).then_inc(rc_ld, 16)
                sp.dma_start(rGN[:, 1], io["gla_out_norm"][l].unsqueeze(0).broadcast_to([P, DV])).then_inc(rc_ld, 16)

                def load_r(u, tok, n, g):
                    sp.dma_start(rQQ[:, u, 0:2, 0:n], zf_d[0:2, :, tok].rearrange("f p t -> p f t")).then_inc(r_ld[u], 16)
                    sp.dma_start(rHF[:, u, :, 0:n], zf_d[2:4, :, tok].rearrange("f p t -> p f t")).then_inc(r_ld[u], 16)
                    sp.dma_start(rQQ[:, u, 2, 0:n], zf_d[4, :, tok]).then_inc(r_ld[u], 16)
                    sp.dma_start(rKK[:, u, 2, 0:n], zf_d[5, :, tok]).then_inc(r_ld[u], 16)
                    sp.dma_start(rV[0:n, u, :, :], zt_d[tok, 512:1536].rearrange("t (a c) -> t a c", a=2)).then_inc(r_ld[u], 16)
                    sp.dma_start(rGA[0:n, u, :], zt_d[tok, ZT_GA:ZT_GA + 16]).then_inc(r_ld[u], 16)

                with sp.Fori(0, 4) as i:
                    for u in range(2):
                        wait(sp, "r_dve", l * 8 + 2 * i + u - 2, "fin")
                        load_r(u, bass.ds((2 * i + u) * P, P), P, None)
                wait(sp, "r_dve", l * 8 + 6, "fin")
                load_r(0, slice(SEQ, TOK), DEC_SEQ, None)
                wait(sp, "r_dve", l * 8 + 7, "fin")
                store_state(sp, l, io["hg_p"], io["gla_p"], 0)
                sp.wait_ge(rs_out, (l * 2 + 1) * 8 * 16)
                wait(sp, "rs_pool", l, "clear")
                for h in range(HG_H):
                    sp.dma_start(rS[64 * (h % 2):64 * (h % 2) + 64, 0, 64 * h:64 * h + 64],
                                 io["state_hgrn"][l][0, h]).then_inc(rs_ld, 16)
                for h in range(GLA_H):
                    sp.dma_start(rS[32 * h:32 * h + 32, 0, 256 + 64 * h:320 + 64 * h],
                                 io["state_gla"][l][0, h]).then_inc(rs_ld, 16)
                wait(sp, "rt_dve", l, "fin")
                store_state(sp, l, io["hg_s"], io["gla_s"], 1)
                for u in range(2):
                    sp.wait_ge(r_out[u], (l * [5, 4][u] + [5, 4][u]) * 16)
                sp.wait_ge(rs_out, (l * 2 + 2) * 8 * 16)

                at = 0
                for name, wd in (("mla_cq_norm", 256), ("mla_ckv_norm", 256), ("mla_q_norm", QK), ("mla_k_norm", QK),
                                 ("mla_out_norm", 512)):
                    sp.dma_start(GN[:, at:at + wd], io[name][l].unsqueeze(0).broadcast_to([P, wd])).then_inc(ac_ld, 16)
                    at += wd
                for t, (t0, n) in enumerate(TILES):
                    if t:
                        wait(sp, "a_dve", l, f"krope{t - 1}_3")
                        wait(sp, "a_dve", l, f"kvn{t - 1}")
                        wait(sp, "a_pe", l, f"cT{t - 1}")
                        wait(sp, "a_pool", l, f"kr{t - 1}")
                    if t == NTILE - 1:
                        for j in range(4):
                            if j:
                                wait(sp, "a_pe", l, f"pcT{j - 1}")
                                wait(sp, "a_dve", l, f"pkm{j - 1}_g")
                                wait(sp, "a_pool", l, f"pkr{j - 1}")
                            else:
                                sp.wait_ge(kv_out, (l * 2 * NTILE + 2 * (NTILE - 1)) * 16)
                            sp.dma_start(ZT[:, 256:512], io["cache_mla_ckv"][l][0, P * j:P * j + P]).then_inc(a_ld, 16)
                            sp.dma_start(ZT[:, 512:544], io["cache_mla_krope"][l][0, P * j:P * j + P]).then_inc(a_ld, 16)
                        wait(sp, "a_pe", l, "pcT3")
                        wait(sp, "a_pool", l, "pkr3")
                    elif t:
                        sp.wait_ge(kv_out, (l * 2 * NTILE + 2 * t) * 16)
                    sp.dma_start(ZT[0:n, 0:512], zt_d[t0:t0 + n, 0:512]).then_inc(a_ld, 16)
                    sp.dma_start(ZT[0:n, 512:544], zt_d[t0:t0 + n, ZT_KR:ZT_KR + 32]).then_inc(a_ld, 16)

                wait(sp, "a_pe", l, f"Q{NTILE - 1}")
                for n in range(3):
                    load_raw(l, 12 + n, w_o_v[l][:, :, 256 * n:256 * n + 256], 8)
                sp.wait_ge(a_out, (l + 1) * NTILE * 16)
                for t, (t0, n) in enumerate(TILES):
                    if t == 0:
                        wait(sp, "a_pe", l, f"PV{NTILE - 1}_7")
                        wait(sp, "a_dve", l, f"on{NTILE - 1}")
                    if t >= 2:
                        wait(sp, "mix_pe", l, f"m{t - 2}b")
                    sp.dma_start(MT[0:n, t % 2], mix_d[t0:t0 + n, :]).then_inc(m_ld[t % 2], 16)
                sp.wait_ge(w_lo, lo_val(l, 9))
                load_raw(l, 15, w_o_v[l][:, :, 768:1024], 8)

                with sp.Fori(0, NGROUP) as i:
                    for j in range(3):
                        sp.wait_ge(w_lo, lo_val(l, 10 + 3 * i + j))
                        if j == 0:
                            load_raw(l, 16, w_f1_v[l][:, :, bass.ds(i * GROUP, GROUP)], 8)
                        elif j == 1:
                            load_raw(l, 17, w_f1_v[l][:, :, bass.ds(i * GROUP + D_FF, GROUP)], 8)
                        else:
                            load_raw(l, 18, w_f2_v[l][:, bass.ds(i * 2, 2), :], 2)

            for t, (t0, n) in enumerate(TILES):
                wait(sp, "out_dve", 0, f"y{t}b")
                sp.dma_start(rows(yp, ys, t), XT[0:n, t % 2]).then_inc(y_out[t % 2], 16)
            sp.wait_ge(y_out[0], 5 * 16)
            sp.wait_ge(y_out[1], 4 * 16)
            sp.wait_ge(kv_out, DEPTH * 2 * NTILE * 16)
            sp.wait_ge(rs_out, DEPTH * 2 * 8 * 16)

        @block.gpsimd
        def _(pool):
            class V:
                @staticmethod
                def tensor_copy(*x):
                    settle(pool)
                    return nc.gpsimd.tensor_copy(*x)

                @staticmethod
                def tensor_tensor(*x):
                    settle(pool)
                    return nc.gpsimd.tensor_tensor(*x)

                @staticmethod
                def memset(*x):
                    settle(pool)
                    return nc.gpsimd.memset(*x)

                @staticmethod
                def dma_start(*x):
                    settle(pool)
                    return nc.gpsimd.dma_start(*x)

            def norm_hi(name, l):
                s = st(name + "_pool")
                for c, (c0, cn) in enumerate(CHUNKS):
                    for k in range(KT8):
                        wait(pool, name + "_act", l, f"h{c}{k}")
                        s.done(V.tensor_copy(A[:, 0, k, c0:c0 + cn], TN[:, k % 2, 0:cn]), f"hi{c}{k}")

            def spill_out(b, dst, src):
                V.dma_start(dst, src).then_inc(spill[b], 16)

            with pool.Fori(0, DEPTH) as l:
                wait(pool, "kg_dve", l, "kglo")
                norm_hi("n1", l)
                for q in range(18):
                    ft, c = q // 3, q % 3
                    c0, cn = CHUNKS[c]
                    wait(pool, "z_act", l, f"f{q}")
                    spill_out(q % 3, zf_d[ft, :, c0:c0 + cn], ZS[:, q % 3, 0:cn])
                for t, (t0, n) in enumerate(TILES):
                    wait(pool, "z_act", l, f"g{t}")
                    spill_out(t % 3, zt_d[t0:t0 + n, 1536:1584], ZS[0:n, t % 3, 0:48])
                for j in range(6):
                    for t, (t0, n) in enumerate(TILES):
                        wait(pool, "z_act", l, f"t{j}_{t}")
                        spill_out(t % 3, zt_d[t0:t0 + n, 256 * j:256 * j + 256], ZS[0:n, t % 3, 0:256])

                for i in range(3):
                    pool.wait_ge(spill[i], (l + 1) * SPILL_N[i] * 16)
                s = st("rs_pool")
                s.done(V.memset(rQX[:], 0.0), "zqx")
                s.done(V.memset(rS[:, 0], 0.0), "zs")
                wait(pool, "rs_pool", l, "zs")

                def recur_pool(kind, g, u, n):
                    s = st(kind + "_pool")
                    s.body()
                    q = rQQ[:, u, :, 0:n]
                    before = []

                    def step(run, name):
                        if before:
                            wait(pool, kind + "_pool", g, before[-1])
                        s.done(run(), name)
                        before.append(name)

                    def expand(b, lv):
                        qx = rQX[:, b, :, 0:n]
                        e = rE[:, b, :, 0:n]
                        for j, (r0, rn, hs, f) in enumerate(
                                [(0, 64, slice(0, 4, 2), slice(0, 2)), (64, 64, slice(1, 4, 2), slice(0, 2))]
                                + [(32 * h, 32, slice(4 + h, 5 + h), slice(2, 3)) for h in range(GLA_H)]):
                            o = qx[r0:r0 + rn, hs, :]
                            if lv == 0:
                                step(lambda: V.tensor_copy(o, q[r0:r0 + rn, f, :]), f"qx0_{j}")
                            else:
                                step(lambda: V.tensor_tensor(o, q[r0:r0 + rn, f, :], e[r0:r0 + rn, f, :], ALU.mult),
                                     f"qx{lv}_{j}")

                    wait(pool, kind + "_dve", g, "qscale")
                    expand(0, 0)
                    for lv in range(1, 7):
                        wait(pool, kind + "_act", g, f"e{lv}")
                        if lv >= 2:
                            wait(pool, kind + "_pe", g, f"s{lv - 2}")
                        expand(lv % 2, lv)
                    wait(pool, kind + "_act", g, "eb")
                    wait(pool, kind + "_pe", g, "s5")
                    step(lambda: V.tensor_tensor(rKE[:, 1, :, 0:n], q, rE[:, 1, :, 0:n], ALU.mult), "qb")
                    wait(pool, kind + "_dve", g, "grec")
                    nh = 4
                    gt = rV[0:n, u, :, 256:512]
                    eg = rEG[0:n].rearrange("p (a c) -> p a c", a=2)
                    step(lambda: V.tensor_tensor(eg, eg, gt, ALU.mult), "gs")
                    for a_ in range(2):
                        e4 = rEG[0:n, 256 * a_:256 * a_ + 256].rearrange("p (h v) -> p h v", h=nh)
                        step(lambda: V.tensor_tensor(e4, e4, rGN[0:n, a_].unsqueeze(1).broadcast_to([n, nh, DV]), ALU.mult),
                             f"gg{a_}")
                    wait(pool, kind + "_dve", g, "fin")

                settle(pool)
                with pool.Fori(0, 4) as i:
                    for u in range(2):
                        g = l * 8 + 2 * i + u
                        recur_pool("r", g, u, P)
                        V.dma_start(mix_d[bass.ds((2 * i + u) * P, P), 512:1024], rOUT[:, u]).then_inc(r_out[u], 16)
                        pool.wait_ge(r_out[u], (l * [5, 4][u] + i + 1) * 16)
                settle(pool)
                pool.wait_ge(rs_out, (l * 2 + 1) * 8 * 16)
                st("rs_pool").done(V.memset(rS[:, 0], 0.0), "clear")
                recur_pool("rt", l, 0, DEC_SEQ)
                V.dma_start(mix_d[SEQ:TOK, 512:1024], rOUT[0:DEC_SEQ, 0]).then_inc(r_out[0], 16)
                pool.wait_ge(r_out[0], (l * 5 + 5) * 16)

                s = st("a_pool")
                for t, (t0, n) in enumerate(TILES):
                    if t == NTILE - 1:
                        for j in range(4):
                            pool.wait_ge(a_ld, (l * 26 + 2 * (NTILE - 1) + 2 * (j + 1)) * 16)
                            if j:
                                wait(pool, "a_pe", l, f"p{j - 1}_KTb")
                            else:
                                wait(pool, "a_pe", l, f"{t - 1}_KTb")
                            s.done(V.tensor_copy(KM[:, :, NOPE:QK],
                                                 ZT[:, 512:544].unsqueeze(1).broadcast_to([P, HEADS, ROPE])), f"pkr{j}")
                        wait(pool, "a_pe", l, "p3_KTb")
                    elif t:
                        wait(pool, "a_pe", l, f"{t - 1}_KTb")
                    wait(pool, "a_dve", l, f"krope{t}_3")
                    V.dma_start(io["ckv_p"][l][0, t0:t0 + n] if t < 8 else io["ckv_s"][l][0], ZT[0:n, 256:512]).then_inc(kv_out, 16)
                    V.dma_start(io["kr_p"][l][0, t0:t0 + n] if t < 8 else io["kr_s"][l][0], ZT[0:n, 512:544]).then_inc(kv_out, 16)
                    s.done(V.tensor_copy(KM[0:n, :, NOPE:QK],
                                         ZT[0:n, 512:544].unsqueeze(1).broadcast_to([n, HEADS, ROPE])), f"kr{t}")
                    wait(pool, "a_dve", l, f"on{t}")
                    V.dma_start(mix_d[t0:t0 + n, 0:512], OM[0:n]).then_inc(a_out, 16)
                norm_hi("n2", l)

        @block.scalar
        def _(act):
            S = nc.scalar

            def split_hi(l, m, free, raw):
                r, rr = m % 3, raw % 3
                act.wait_ge(raw_ld[rr], raw_ready(l, raw))
                free()
                S.activation(W[:, r, 0], WR[:, rr], ACT.Copy).then_inc(w_hi, 1)

            def norm(name, l, sh):
                s = st(name + "_act")
                for c, (c0, cn) in enumerate(CHUNKS):
                    for k in range(KT8):
                        q = c * KT8 + k
                        if q >= 2:
                            wait(act, name + "_pe", l, f"q{(q - 2) // 8}{(q - 2) % 8}")
                        s.done(S.activation(SQ[:, k % 2, 0:cn], X[:, k, c0:c0 + cn], ACT.Square), f"sq{c}{k}")
                    wait(act, name + "_pe", l, f"q{c}7")
                    if c:
                        wait(act, name + "_dve", l, f"t{c - 1}7")
                    s.done(S.activation(RS[:, 0:cn], ps[3 + c][:, 0:cn], ACT.Ln, bias=EPSC), f"rl{c}")
                    wait(act, name + "_act", l, f"rl{c}")
                    s.done(S.activation(RS[:, 0:cn], RS[:, 0:cn], ACT.Exp, scale=-0.5), f"rs{c}")
                    for k in range(KT8):
                        wait(act, name + "_dve", l, f"t{c}{k}")
                        parts = [(0, cn, 0)] if c < 2 else [(0, 256, 0), (256, 320, 1)]
                        for j, (a0, a1, m) in enumerate(parts):
                            ins = S.activation(TN[:, k % 2, a0:a1], TN[:, k % 2, a0:a1], ACT.Identity,
                                               bias=MOD[:, sh + k, m:m + 1], scale=GS[:, k, m:m + 1])
                            s.done(ins, f"h{c}{k}" if j == len(parts) - 1 else f"h{c}{k}p")

            def rsqrt(s, view, parts, n, name, own):
                for j, (v, width) in enumerate(parts):
                    s.done(S.activation(v, v, ACT.Ln, bias=EPSC[0:n], scale=1.0 / width), f"{name}l{j}")
                own(f"{name}l{len(parts) - 1}")
                s.done(S.activation(view, view, ACT.Exp, scale=-0.5), name)

            table = "natural_log_exp_and_others"
            S.preload_act_table_set(table)
            wait(act, "in_pe", 0, "rows")
            s = st("in_act")
            s.done(S.activation(SM[:, 0:16], ps[7][:, 0:16], ACT.Exp, scale=-1.0), "ec")
            for t, (t0, n) in enumerate(TILES):
                for b in range(2):
                    wait(act, "in_pe", 0, f"x{t}{'ab'[b]}")
                    src = ps[2 * (t % 2) + b][:, 0:512].rearrange("p (k t) -> p k t", k=4)[:, :, 0:n]
                    s.done(S.activation(X[:, 4 * b:4 * b + 4, t0:t0 + n], src, ACT.Copy), f"x{t}{'ab'[b]}")
            wait(act, "in_dve", 0, "s1")
            st("lb_act").done(S.activation(SM[:, 42:46], SM[:, 42:46], ACT.Exp), "exp")

            with act.Fori(0, DEPTH) as l:
                S.preload_act_table_set(table)
                wait(act, "ffn_dve", l * NGROUP - 1, "x23")
                act.dma_start(PRR[0:48, :], io["b_mod"][l].rearrange("(k p) -> k p", p=P)).then_inc(par_ld, 16)
                act.dma_start(PRR[48:56, :], io["norm_mix"][l].rearrange("(k p) -> k p", p=P)).then_inc(par_ld, 16)
                act.dma_start(PRR[56:64, :], io["norm_ffn"][l].rearrange("(k p) -> k p", p=P)).then_inc(par_ld, 16)
                act.dma_start(PRR[64:65, :], io["gla_b_a"][l].unsqueeze(0)).then_inc(par_ld, 16)
                act.dma_start(WA2[:], io["gla_w_a2"][l]).then_inc(par_ld, 16)
                act.dma_start(KGW[:, :, 0:32], w_in_v[l][:, :, C_KR:C_KR + 32]).then_inc(par_ld, 16)
                act.dma_start(KGW[:, :, 32:48], w_in_v[l][:, :, C_GA:C_GA + 16]).then_inc(par_ld, 16)

                def ffn_free():
                    wait(act, "ffn_pe", l * NGROUP - 1, "x23")
                for m in range(3):
                    split_hi(l, m, ffn_free, m)
                act.wait_ge(par_ld, (l + 1) * 7 * 16)
                s = st("z_act")
                s.done(S.activation(KGS[:, 0], KGW[:], ACT.Copy), "kghi")
                norm("n1", l, 0)
                for q in range(18):
                    wait(act, "zf_pe", l, f"f{q}")
                    cn = CHUNKS[q % 3][1]
                    if q >= 3:
                        act.wait_ge(spill[q % 3], (l * 27 + q // 3) * 16)
                    else:
                        wait(act, "n1_dve", l, "lo27")
                        wait(act, "n1_pool", l, "hi27")
                    s.done(S.activation(ZS[:, q % 3, 0:cn], ps[q % 3][:, 0:cn], ACT.Copy), f"f{q}")
                    if q % 6 == 5:
                        m = q // 6 + 3
                        split_hi(l, m, lambda: wait(act, "zf_pe", l, f"f{q}"), m)
                for t, (t0, n) in enumerate(TILES):
                    wait(act, "zf_pe", l, f"g{t}")
                    act.wait_ge(spill[t % 3], (l * 27 + 6 + t // 3) * 16)
                    s.done(S.activation(ZS[0:n, t % 3, 0:48], ps[t % 3][0:n, 0:48], ACT.Copy), f"g{t}")
                for j in range(6):
                    for t, (t0, n) in enumerate(TILES):
                        turn = l * 2 + j // 3
                        wait(act, "zt_pe", turn, f"t{j % 3}_{t}")
                        act.wait_ge(spill[t % 3], (l * 27 + 9 + 3 * j + t // 3) * 16)
                        s.done(S.activation(ZS[0:n, t % 3, 0:256], ps[t % 3][0:n, 0:256], ACT.Copy), f"t{j}_{t}")
                    if j < 3:
                        split_hi(l, j + 6, lambda: wait(act, "zt_pe", l * 2 + j // 3, f"t{j % 3}_8"), j + 6)

                act.wait_ge(rc_ld, (l + 1) * 48)

                def recur_act(kind, g, u, n, loaded):
                    s = st(kind + "_act")
                    s.body()
                    act.wait_ge(r_ld[u], loaded)
                    wait(act, kind + "_pe", g, "gaT")
                    s.done(S.activation(rGT[:, 0:n], ps[6][0:16, 0:n], ACT.Copy), "gaT")
                    s.done(S.activation(rT1[:, :, 0:n], rHF[:, u, :, 0:n], ACT.Exp, scale=-1.0), "ehf")
                    wait(act, kind + "_pe", g, "gate")
                    s.done(S.activation(rT2[:, 0:n], ps[7][:, 0:n], ACT.Abs, bias=PRM[:, 64:65]), "abs")
                    wait(act, kind + "_act", g, "abs")
                    s.done(S.activation(rT2[:, 0:n], rT2[:, 0:n], ACT.Exp, scale=-1.0), "eabs")
                    wait(act, kind + "_act", g, "eabs")
                    s.done(S.activation(rT2[:, 0:n], rT2[:, 0:n], ACT.Ln, bias=1.0), "labs")
                    wait(act, kind + "_dve", g, "fmax")
                    s.done(S.activation(rG[:, 0:2, 0:n], rT1[:, :, 0:n], ACT.Ln), "lnf")
                    for lv in range(1, 7):
                        wait(act, kind + "_dve", g, f"d{lv}l")
                        if lv >= 3:
                            wait(act, kind + "_dve", g, f"ke{lv - 2}")
                            wait(act, kind + "_pool", g, f"qx{lv - 2}_5")
                        s.done(S.activation(rE[:, lv % 2, :, 0:n], rD[:, lv % 2, :, 0:n], ACT.Exp), f"e{lv}")
                    wait(act, kind + "_dve", g, "dl1" if n == P else "dl0")
                    wait(act, kind + "_dve", g, "ke5")
                    wait(act, kind + "_pool", g, "qx5_5")
                    s.done(S.activation(rE[:, 1, :, 0:n], rB[:, :, 0:n], ACT.Exp), "eb")
                    wait(act, kind + "_dve", g, "ke6")
                    wait(act, kind + "_pool", g, "qx6_5")
                    s.done(S.activation(rE[:, 0, :, 0:n], rD[:, 1, :, 0:n], ACT.Exp), "el")
                    eg = rEG[0:n].rearrange("p (a c) -> p a c", a=2)
                    s.done(S.activation(eg, rV[0:n, u, :, 256:512], ACT.Exp, scale=-1.0), "eg")
                    wait(act, kind + "_pe", g, "klT")
                    s.done(S.activation(rKT[0:n], ps[4][0:n, 0:384].rearrange("p (f k) -> p f k", f=3), ACT.Copy), "klT")
                    wait(act, kind + "_pe", g, "o")
                    s.done(S.activation(rO[0:n], ps[7][0:n], ACT.Square), "osq")
                    wait(act, kind + "_dve", g, "oss")
                    rsqrt(s, rSS[0:n], [(rSS[0:n], DV)], n, "or", lambda x: wait(act, kind + "_act", g, x))
                    wait(act, kind + "_dve", g, "fin")

                with act.Fori(0, 4) as i:
                    S.preload_act_table_set(table)
                    for u in range(2):
                        recur_act("r", l * 8 + 2 * i + u, u, P, (l * [5, 4][u] + i + 1) * 96)
                S.preload_act_table_set(table)
                recur_act("rt", l, 0, DEC_SEQ, (l * 5 + 5) * 96)

                s = st("a_act")
                act.wait_ge(ac_ld, (l + 1) * 80)

                def own(step):
                    wait(act, "a_act", l, step)

                def k_side(tag, n, pos):
                    wait(act, "a_pe", l, f"{tag}K")
                    s.done(S.activation(QSQ[0:n, 0:512], ps[0][0:n], ACT.Square), f"{tag}ksq")
                    wait(act, "a_pe", l, f"{tag}V" if tag[0] == "p" else f"V{tag[:-1]}")
                    s.done(S.activation(Vt[0:n, pos], ps[1][0:n], ACT.Copy), f"{tag}v")
                    wait(act, "a_dve", l, f"kss{tag[:-1]}")
                    rsqrt(s, AS[0:n, 3:11], [(AS[0:n, 3:11], NOPE)], n, f"{tag}kr", own)
                    for b in range(2):
                        wait(act, "a_pe", l, f"{tag}KTb" if b else f"{tag}KTa")
                        src = ps[2 + b][0:QK].rearrange("p (h t) -> p h t", h=4)[:, :, 0:n]
                        s.done(S.activation(KTt[:, 4 * b:4 * b + 4, P * pos:P * pos + n], src, ACT.Copy), f"{tag}kt{b}")

                for t, (t0, n) in enumerate(TILES):
                    if t == NTILE - 1:
                        for j in range(4):
                            wait(act, "a_pe", l, f"pcT{j}")
                            s.done(S.activation(CT[:, 2:4, 0:P], ps[4][:, 256:512].rearrange("p (k t) -> p k t", k=2),
                                                ACT.Copy), f"pcT{j}")
                            k_side(f"p{j}_", P, j)
                    pos = t if t < 8 else 4
                    act.wait_ge(a_ld, (l * 26 + 2 * (t + 1) + (8 if t == 8 else 0)) * 16)
                    if t:
                        wait(act, "a_dve", l, f"on{t - 1}")
                    for j, (c0, c1) in enumerate(((0, 256), (256, 512), (512, 544))):
                        s.done(S.activation(QSQ[0:n, 0:c1 - c0], ZT[0:n, c0:c1], ACT.Square,
                                            accum_out=AS[0:n, j:j + 1]), f"zsq{t}_{j}")
                        own(f"zsq{t}_{j}")
                    rsqrt(s, AS[0:n, 0:3], [(AS[0:n, 0:2], RANK), (AS[0:n, 2:3], ROPE)], n, f"zr{t}", own)
                    wait(act, "a_pe", l, f"cT{t}")
                    s.done(S.activation(CT[:, :, 0:n], ps[4][:].rearrange("p (k t) -> p k t", k=4)[:, :, 0:n], ACT.Copy),
                           f"cT{t}")
                    k_side(f"{t}_", n, pos)
                    wait(act, "a_pe", l, f"Q{t}")
                    wait(act, "a_dve", l, f"kss{t}")
                    for b in range(2):
                        s.done(S.activation(QSQ[0:n, 384 * b:384 * b + 384], ps[5 + b][0:n, 0:384], ACT.Square), f"qsq{t}_{b}")
                    wait(act, "a_dve", l, f"qs{t}b")
                    rsqrt(s, AS[0:n, 3:19], [(AS[0:n, 3:11], NOPE), (AS[0:n, 11:19], ROPE)], n, f"qr{t}", own)
                    for b in range(2):
                        wait(act, "a_pe", l, f"QT{t}_{b}")
                        src = ps[2 + b][0:QK].rearrange("p (h t) -> p h t", h=4)[:, :, 0:n]
                        s.done(S.activation(QT[:, 4 * b:4 * b + 4, 0:n], src, ACT.Copy), f"qt{t}_{b}")
                    keys = P * (t + 1) if t < 8 else PAST + DEC_SEQ
                    for h in range(HEADS):
                        b0 = 2 * (h % 2)
                        wait(act, "a_dve", l, f"mx{t}_{h}n")
                        if h >= 2:
                            wait(act, "a_pe", l, f"T{t}_{h - 2}")
                        parts = [(0, min(512, keys))] + ([(512, keys)] if keys > 512 else [])
                        for j, (k0, k1) in enumerate(parts):
                            s.done(S.activation(PB[0:n, h % 2, k0:k1], ps[b0 + j][0:n, 0:k1 - k0], ACT.Exp,
                                                bias=AS[0:n, 24 + h:25 + h], scale=MLA_SCALE,
                                                accum_out=AS[0:n, 32 + 2 * h + j:33 + 2 * h + j]), f"p{t}_{h}_{j}")
                    wait(act, "a_dve", l, f"on0{t}")
                    s.done(S.activation(QSQ[0:n, 0:512], OM[0:n], ACT.Square, accum_out=AS[0:n, 48:49]), f"osq{t}")
                    own(f"osq{t}")
                    rsqrt(s, AS[0:n, 48:49], [(AS[0:n, 48:49], MLA_W)], n, f"or{t}", own)

                s = st("mix_act")
                for t, (t0, n) in enumerate(TILES):
                    for b in range(2):
                        wait(act, "mix_pe", l, f"m{t}{'ab'[b]}")
                        src = ps[2 * (t % 2) + b][:].rearrange("p (k t) -> p k t", k=4)[:, :, 0:n]
                        s.done(S.activation(A[:, 0, 4 * b:4 * b + 4, t0:t0 + n], src, ACT.Copy), f"m{t}{'ab'[b]}")
                for m in range(9, 12):
                    split_hi(l, m, lambda: None, m + 3)
                split_hi(l, 12, lambda: wait(act, "wo_pe", l, "o5"), 15)
                for j in range(3):
                    split_hi(l, 13 + j, lambda: wait(act, "wo_pe", l, f"o{[11, 17, 23][j]}"), 16 + j)
                norm("n2", l, 24)

                def group(g, i, last):
                    s = st("ffn_act")
                    s.body()
                    for p in range(6):
                        cn = CHUNKS[p % 3][1]
                        c0 = CHUNKS[p % 3][0]
                        wait(act, "ffn_pe", g, f"a{p}")
                        if p >= 2:
                            wait(act, "ffn_dve", g, f"mul{p - 2}")
                        s.done(S.activation(SIL[:, p % 2, 0:cn], ps[2 * (p % 3)][:, 0:cn], ACT.Silu), f"sil{p}")
                        if p == 0:
                            wait(act, "ffn_pe", g - 1, "x23")
                        wait(act, "ffn_dve", g, f"mul{p}")
                        s.done(S.activation(HID[:, 0, p // 3, c0:c0 + cn], HF32[:, p % 2, 0:cn], ACT.Copy), f"hi{p}")
                    for j in range(3):
                        wait(act, "ffn_pe", g, "u5" if j < 2 else "x23")
                        if not last:
                            act.wait_ge(raw_ld[(16 + j) % 3], (l * raw_cnt[(16 + j) % 3] + (19 + j) // 3 + i + 1) * 16)
                            S.activation(W[:, (13 + j) % 3, 0], WR[:, (16 + j) % 3], ACT.Copy).then_inc(w_hi, 1)

                with act.Fori(0, NGROUP - 1) as i:
                    group(l * NGROUP + i, i, False)
                group(l * NGROUP + NGROUP - 1, NGROUP - 1, True)

        @block.tensor
        def _(pe):
            T = nc.tensor

            def transpose(*x):
                settle(pe)
                return T.transpose(*x)
            PASSES = ((0, 0), (0, 1), (1, 0))

            def mm(out, lhsT, rhs, start, stop):
                return T.matmul(out, lhsT, rhs, start=start, stop=stop, skip_group_check=True)

            def norm(name, l):
                st_ = st(name + "_pe")
                for c, (c0, cn) in enumerate(CHUNKS):
                    for k in range(KT8):
                        wait(pe, name + "_act", l, f"sq{c}{k}")
                        ins = mm(ps[3 + c][:, 0:cn], CST[:, O_ONES:O_ONES + P], SQ[:, k % 2, 0:cn], k == 0, k == KT8 - 1)
                        st_.done(ins, f"q{c}{k}")

            prime(pe, "ffn_pe")
            pe.wait_ge(setup_ld, 64)
            s = st("in_pe")
            s.done(transpose(ps[7][:, 0:20], PRR[0:20, :], CST[0:20, 0:20]), "rows")

            def turn_in(src, t, n, s, names, bank):
                for k in range(8):
                    ins = transpose(ps[bank + k // 4][:, P * (k % 4):P * (k % 4) + n], src[0:n, P * k:P * k + P],
                                      CST[0:n, 0:n])
                    if k % 4 == 3:
                        s.done(ins, names[k // 4])

            for t, (t0, n) in enumerate(TILES):
                pe.wait_ge(x_ld[t % 2], 16 * (t // 2 + 1))
                if t >= 2:
                    wait(pe, "in_act", 0, f"x{t - 2}b")
                turn_in(XT[:, t % 2], t, n, s, (f"x{t}a", f"x{t}b"), 2 * (t % 2))

            with pe.Fori(0, DEPTH) as l:
                s = st("par_pe")
                pe.wait_ge(par_ld, (l + 1) * 112)
                wait(pe, "in_dve", 0, "lbd")
                s.done(transpose(ps[5][:, 0:65], PRR[0:65, :], CST[0:65, 0:65]), "rows")

                def mod_slot(s, round_=0, rounds=0, step=0):
                    pe.wait_ge(mod_ld[s % 2], (l * 12 + s // 2 + 1 + round_ * (step // 2)) * 16)
                    if s >= 2:
                        pe.wait_ge(mod_dve, l * NMOD + s - 1 + round_ * step)
                    w = MR[:, s % 2].rearrange("p (k c) -> p k c", k=8)
                    for ct in range(2):
                        for k in range(KT8):
                            ins = mm(ps[6 + s % 2][:, 2 * ct:2 * ct + 2], w[:, k, P * ct:P * ct + P], SCV[:, k, :],
                                     k == 0, k == KT8 - 1)
                    ins.then_inc(mod_pe, 1)

                wait(pe, "in_dve", 0, "sc")
                for q in range(8):
                    mod_slot(q)
                wait(pe, "par_dve", l, "prm")
                norm("n1", l)

                s = st("zf_pe")

                def split_ready(m):
                    pe.wait_ge(w_lo, lo_val(l, m))

                for m in range(3):
                    for ct in range(2):
                        for c, (c0, cn) in enumerate(CHUNKS):
                            q = 6 * m + 3 * ct + c
                            if q < 3:
                                wait(pe, "n1_dve", l, f"lo{c}7")
                            if ct == 0 and c == 0:
                                split_ready(m)
                            if q >= 3:
                                wait(pe, "z_act", l, f"f{q - 3}")
                            for k in range(KT8):
                                w = W[:, m, :, :].rearrange("p a (k c) -> p a k c", k=8)
                                for j, (wa, xa) in enumerate(PASSES):
                                    ins = mm(ps[q % 3][:, 0:cn], w[:, wa, k, P * ct:P * ct + P], A[:, xa, k, c0:c0 + cn],
                                             k == 0 and j == 0, k == KT8 - 1 and j == 2)
                            s.done(ins, f"f{q}")

                def token_major(out, rhs, t0, n, width):
                    for k in range(KT8):
                        for j, (wa, xa) in enumerate(PASSES):
                            ins = mm(out[0:n, 0:width], A[:, xa, k, t0:t0 + n], rhs(wa, k), k == 0 and j == 0,
                                     k == KT8 - 1 and j == 2)
                    return ins

                wait(pe, "kg_dve", l, "kglo")
                for t, (t0, n) in enumerate(TILES):
                    wait(pe, "z_act", l, f"f{15 + t}" if t < 3 else f"g{t - 3}")
                    s.done(token_major(ps[t % 3], lambda wa, k: KGS[:, wa, k, :], t0, n, 48), f"g{t}")
                for q in range(8, 12):
                    mod_slot(q)
                s = st("zt_pe")
                settle(pe)
                with pe.Fori(0, 2) as i:
                    turn = l * 2 + i
                    for j in range(3):
                        pe.wait_ge(w_lo, lo_val(l, 3 + j) + 3 * i)
                        for t, (t0, n) in enumerate(TILES):
                            za = st("z_act")
                            if t >= 3:
                                pe.wait_ge(za.sem, za.value(l, f"t{j}_{t - 3}") + 27 * i)
                            elif j:
                                pe.wait_ge(za.sem, za.value(l, f"t{j - 1}_{t + 6}") + 27 * i)
                            else:
                                pe.wait_ge(za.sem, za.value(l, f"g{t + 6}") + 27 * i)
                            s.done(token_major(ps[t % 3],
                                               lambda wa, k: W[:, j, wa, 256 * k:256 * k + 256], t0, n, 256), f"t{j}_{t}")
                    for q in range(6):
                        mod_slot(12 + q, i, 2, 6)

                pe.wait_ge(rc_ld, (l + 1) * 48)
                pe.wait_ge(mod_dve, (l + 1) * NMOD)
                wait(pe, "rs_pool", l, "zs")

                def recur_pe(kind, g, u, n, loaded):
                    s = st(kind + "_pe")
                    s.body()
                    nc_ = n // CHUNK
                    pe.wait_ge(r_ld[u], loaded)
                    s.done(transpose(ps[6][0:16, 0:n], rGA[0:n, u], CST[0:n, 0:n]), "gaT")
                    wait(pe, kind + "_act", g, "gaT")
                    s.done(mm(ps[7][:, 0:n], WA2[:], rGT[:, 0:n], True, True), "gate")
                    for lv in range(7):
                        wait(pe, kind + "_pool", g, f"qx{lv}_5")
                        if lv == 0:
                            wait(pe, kind + "_dve", g, "k01")
                        else:
                            wait(pe, kind + "_dve", g, f"ke{lv}")
                        if lv >= 2:
                            wait(pe, kind + "_dve", g, f"pr{lv - 2}b")
                        b = 2 * (lv % 2)
                        k = rKK[:, u] if lv == 0 else rKE[:, lv % 2]
                        x = rQX[:, lv % 2]
                        for f, (h0, nh) in enumerate(((0, 2), (2, 2), (4, 4))):
                            out = ps[b + h0 // 4][0:n].rearrange("p (h t) -> p h t", h=4)[:, h0 % 4:h0 % 4 + nh, 0:n]
                            ins = mm(out, k[:, f, 0:n], x[:, h0:h0 + nh, 0:n], h0 % 4 == 0, f > 0)
                        s.done(ins, f"s{lv}")
                    wait(pe, kind + "_dve", g, "kl")
                    for f in range(3):
                        ins = transpose(ps[4][0:n, P * f:P * f + P], rKE[:, 0, f, 0:n], ident)
                    s.done(ins, "klT")
                    wait(pe, kind + "_act", g, "klT")
                    v = rV[:, u, :, 0:256]
                    for c in range(nc_):
                        r0 = CHUNK * c
                        for f, (o0, on, vi, v0) in enumerate(((0, 128, 0, 0), (128, 128, 0, 128), (256, 256, 1, 0))):
                            ins = mm(ps[5 + c][:, o0:o0 + on], rKT[r0:r0 + CHUNK, f, :], v[r0:r0 + CHUNK, vi, v0:v0 + on],
                                     f == 0, f == 2)
                        s.done(ins, f"ds{c}")
                    wait(pe, kind + "_dve", g, "pr6b")
                    settle(pe)
                    for h in range(8):
                        mm(ps[7][0:n, 64 * h:64 * h + 64], rP[0:n, h, 0:n],
                           v[0:n, h // 4, 64 * (h % 4):64 * (h % 4) + 64], h == 0, False)
                    wait(pe, kind + "_pool", g, "qb")
                    for c in range(nc_):
                        if c:
                            wait(pe, kind + "_dve", g, "st0c")
                        for f, (o0, on) in enumerate(((0, 128), (128, 128), (256, 256))):
                            ins = mm(ps[7][CHUNK * c:CHUNK * c + CHUNK, o0:o0 + on],
                                     rKE[:, 1, f, CHUNK * c:CHUNK * c + CHUNK], rS[:, c, o0:o0 + on],
                                     False, c == nc_ - 1 and f == 2)
                        if c < nc_ - 1:
                            s.done(ins, f"o{c}")
                    s.done(ins, "o")
                    wait(pe, kind + "_dve", g, "fin")
                    settle(pe)

                settle(pe)
                with pe.Fori(0, 4) as i:
                    for u in range(2):
                        recur_pe("r", l * 8 + 2 * i + u, u, P, (l * [5, 4][u] + i + 1) * 96)
                pe.wait_ge(rs_ld, (l + 1) * 128)
                recur_pe("rt", l, 0, DEC_SEQ, (l * 5 + 5) * 96)

                s = st("a_pe")
                for j in range(9, 12):
                    pe.wait_ge(raw_ld[j % 3], raw_ready(l, j))

                def lowrank(bank, ci, w, c0, cn, n):
                    for k in range(2):
                        ins = mm(ps[bank][0:n, 0:cn], CT[:, ci + k, 0:n], w[:, k, c0:c0 + cn], k == 0, k == 1)
                    return ins

                def heads_t(src, n, tag):
                    for h in range(HEADS):
                        ins = transpose(ps[2 + h // 4][0:QK, P * (h % 4):P * (h % 4) + n], src[0:n, h, :], CST[0:n, 0:n])
                        if h % 4 == 3:
                            s.done(ins, tag[h // 4])

                def k_side(tag, n, vname):
                    s.done(lowrank(0, 2, WK, 0, 512, n), f"{tag}K")
                    s.done(lowrank(1, 2, WV, 0, 512, n), vname)

                prev_o = None
                for t, (t0, n) in enumerate(TILES):
                    if t:
                        wait(pe, "a_dve", l, f"on0{t - 1}")
                    if t == NTILE - 1:
                        for j in range(4):
                            pe.wait_ge(a_ld, (l * 26 + 2 * (NTILE - 1) + 2 * (j + 1)) * 16)
                            if j:
                                wait(pe, "a_act", l, f"p{j - 1}_kt1")
                                wait(pe, "a_dve", l, f"pkm{j - 1}_g")
                            for k in range(2):
                                ins = transpose(ps[4][:, 256 + P * k:256 + P * k + P],
                                                  ZT[:, 256 + P * k:384 + P * k], ident)
                            s.done(ins, f"pcT{j}")
                            wait(pe, "a_act", l, f"pcT{j}")
                            k_side(f"p{j}_", P, f"p{j}_V")
                            wait(pe, "a_dve", l, f"pkm{j}_g")
                            wait(pe, "a_pool", l, f"pkr{j}")
                            heads_t(KM, P, (f"p{j}_KTa", f"p{j}_KTb"))
                        wait(pe, "a_act", l, "p3_kt1")
                    wait(pe, "a_dve", l, f"kvn{t}")
                    wait(pe, "a_dve", l, f"cqn{t}")
                    if t:
                        wait(pe, "a_act", l, f"osq{t - 1}")
                    for k in range(4):
                        ins = transpose(ps[4][:, P * k:P * k + n], ZT[0:n, P * k:P * k + P], CST[0:n, 0:n])
                    s.done(ins, f"cT{t}")
                    wait(pe, "a_act", l, f"cT{t}")
                    k_side(f"{t}_", n, f"V{t}")
                    for b in range(2):
                        ins = lowrank(5 + b, 0, WQ, 384 * b, 384, n)
                    s.done(ins, f"Q{t}")
                    wait(pe, "a_dve", l, f"km{t}_g")
                    wait(pe, "a_pool", l, f"kr{t}")
                    heads_t(KM, n, (f"{t}_KTa", f"{t}_KTb"))
                    wait(pe, "a_act", l, f"{t}_kt1")
                    wait(pe, "a_dve", l, f"qrope{t}_3")
                    heads_t(QM, n, (f"QT{t}_0", f"QT{t}_1"))
                    wait(pe, "a_act", l, f"qt{t}_1")
                    keys = P * (t + 1) if t < 8 else PAST + DEC_SEQ
                    nk = -(-keys // P)

                    def scores(h):
                        b0 = 2 * (h % 2)
                        if h >= 2:
                            wait(pe, "a_act", l, f"p{t}_{h - 2}_{1 if keys > 512 else 0}")
                        for j, k0 in enumerate(range(0, keys, 512)):
                            kn = min(512, keys - k0)
                            last = k0 + kn == keys
                            ins = mm(ps[b0 + j][0:n, 0:kn], QT[:, h, 0:n], KTt[:, h, k0:k0 + kn], True,
                                     not last or t == 8)
                        if t < 8:
                            d0 = (keys - P) % 512
                            ins = mm(ps[b0 + (keys - P) // 512][:, d0:d0 + P], CST[:, O_MQ:O_MQ + P],
                                     CST[:, O_MK:O_MK + P], False, True)
                        s.done(ins, f"S{t}_{h}")

                    def turn(h):
                        wait(pe, "a_act", l, f"p{t}_{h}_{1 if keys > 512 else 0}")
                        if h:
                            wait(pe, "a_dve", l, f"pt{t}_{h - 1}_{1 if nk > 4 else 0}")
                        for k in range(nk):
                            kn = min(P, keys - P * k)
                            ins = transpose(ps[4 + k // 4][0:kn, P * (k % 4):P * (k % 4) + n],
                                              PB[0:n, h % 2, P * k:P * k + kn], CST[0:n, 0:n])
                        s.done(ins, f"T{t}_{h}")

                    def values(h):
                        wait(pe, "a_dve", l, f"pt{t}_{h}_{1 if nk > 4 else 0}")
                        for k in range(nk):
                            kn = min(P, keys - P * k)
                            ins = mm(ps[7][0:n, 64 * h:64 * h + 64], PT[0:kn, h % 2, k, 0:n],
                                     Vt[0:kn, k, 64 * h:64 * h + 64], k == 0, k == nk - 1)
                        s.done(ins, f"PV{t}_{h}")

                    scores(0)
                    for h in range(HEADS):
                        if h + 1 < HEADS:
                            scores(h + 1)
                        turn(h)
                        if h:
                            values(h - 1)
                    values(HEADS - 1)

                s = st("mix_pe")
                for t, (t0, n) in enumerate(TILES):
                    pe.wait_ge(m_ld[t % 2], (l * [5, 4][t % 2] + t // 2 + 1) * 16)
                    if t >= 2:
                        wait(pe, "mix_dve", l, f"m{t - 2}b")
                    turn_in(MT[:, t % 2], t, n, s, (f"m{t}a", f"m{t}b"), 2 * (t % 2))
                s = st("wo_pe")
                wait(pe, "mix_dve", l, "m8b")
                for m in range(4):
                    split_ready(9 + m)
                    w = W[:, (9 + m) % 3].rearrange("p a (k c) -> p a k c", k=8)
                    for ct in range(2):
                        for c, (c0, cn) in enumerate(CHUNKS):
                            q = 6 * m + 3 * ct + c
                            if q >= 6:
                                wait(pe, "wo_dve", l, f"o{q - 6}")
                            for k in range(KT8):
                                for j, (wa, xa) in enumerate(PASSES):
                                    ins = mm(ps[q % 6][:, 0:cn], w[:, wa, k, P * ct:P * ct + P], A[:, xa, k, c0:c0 + cn],
                                             k == 0 and j == 0, k == KT8 - 1 and j == 2)
                            s.done(ins, f"o{q}")
                wait(pe, "wo_dve", l, "o23")
                norm("n2", l)

                for c in range(3):
                    wait(pe, "n2_dve", l, f"lo{c}7")
                s = st("ffn_pe")
                settle(pe)
                with pe.Fori(0, NGROUP) as i:
                    g = l * NGROUP + i
                    for j in range(2):
                        for c, (c0, cn) in enumerate(CHUNKS):
                            p = 3 * j + c
                            if p == 0:
                                for q in range(2):
                                    pe.wait_ge(w_lo, lo_val(l, 13 + q) + 3 * i)
                            if p < 3:
                                wait(pe, "ffn_dve", g - 1, f"x{19 + 2 * p}")
                            else:
                                wait(pe, "ffn_dve", g, f"mul{p - 3}")
                            for half in range(2):
                                w = W[:, (13 + half) % 3].rearrange("p a (k c) -> p a k c", k=8)
                                for k in range(KT8):
                                    for jj, (wa, xa) in enumerate(PASSES):
                                        ins = mm(ps[2 * (p % 3) + half][:, 0:cn], w[:, wa, k, P * j:P * j + P],
                                                 A[:, xa, k, c0:c0 + cn], k == 0 and jj == 0, k == KT8 - 1 and jj == 2)
                                s.done(ins, f"{'au'[half]}{p}")
                    pe.wait_ge(w_lo, lo_val(l, 15) + 3 * i)
                    w = W[:, 15 % 3].rearrange("p a (k c) -> p a k c", k=2)
                    for d in range(KT8):
                        for c, (c0, cn) in enumerate(CHUNKS):
                            q = 3 * d + c
                            if d == 0:
                                wait(pe, "ffn_dve", g, f"lo{3 + c}")
                            if q < 6:
                                wait(pe, "ffn_dve", g, f"mul{3 + q // 2}")
                            else:
                                wait(pe, "ffn_dve", g, f"x{q - 6}")
                            for k in range(2):
                                for jj, (wa, xa) in enumerate(PASSES):
                                    ins = mm(ps[q % 6][:, 0:cn], w[:, wa, k, P * d:P * d + P], HID[:, xa, k, c0:c0 + cn],
                                             k == 0 and jj == 0, k == 1 and jj == 2)
                            s.done(ins, f"x{q}")
                wait(pe, "ffn_dve", l * NGROUP + NGROUP - 1, "x23")
                settle(pe)

            s = st("out_pe")
            for t, (t0, n) in enumerate(TILES):
                b = 2 * (t % 2)
                if t >= 2:
                    wait(pe, "out_dve", 0, f"y{t - 2}b")
                for k in range(8):
                    ins = transpose(ps[b + k // 4][0:n, P * (k % 4):P * (k % 4) + P], X[:, k, t0:t0 + n], ident)
                    if k % 4 == 3:
                        s.done(ins, f"y{t}{'ab'[k // 4]}")

        @block.vector
        def _(dve):
            V = nc.vector

            def own(name, turn, step):
                wait(dve, name, turn, step)

            def split_lo(l, m, raw):
                dve.wait_ge(w_hi, hi_val(l, m))
                V.tensor_tensor(W[:, m % 3, 1], WR[:, raw % 3], W[:, m % 3, 0].bitcast(F32), ALU.subtract).then_inc(w_lo, 1)

            def norm(name, l, sc, gain):
                s = st(name + "_dve")
                for m in range(2):
                    s.done(V.scalar_tensor_tensor(out=GS[:, :, m], in0=MOD[:, sc:sc + 8, m], scalar=1.0,
                                                  in1=PRM[:, gain:gain + 8], op0=ALU.add, op1=ALU.mult), f"gs{m}")
                for c, (c0, cn) in enumerate(CHUNKS):
                    wait(dve, name + "_act", l, f"rs{c}")
                    for k in range(KT8):
                        q = KT8 * c + k
                        if q >= 2:
                            c2, k2 = (q - 2) // 8, (q - 2) % 8
                            wait(dve, name + "_pool", l, f"hi{c2}{k2}")
                            own(name + "_dve", l, f"lo{c2}{k2}")
                        s.done(V.tensor_tensor(TN[:, k % 2, 0:cn], X[:, k, c0:c0 + cn], RS[:, 0:cn], ALU.mult), f"t{c}{k}")
                        if k:
                            low(name, l, s, c, k - 1)
                    low(name, l, s, c, KT8 - 1)

            def low(name, l, s, c, k):
                c0, cn = CHUNKS[c]
                wait(dve, name + "_pool", l, f"hi{c}{k}")
                s.done(V.tensor_tensor(A[:, 1, k, c0:c0 + cn], TN[:, k % 2, 0:cn],
                                       A[:, 0, k, c0:c0 + cn].bitcast(F32), ALU.subtract), f"lo{c}{k}")

            def residual(s, name, d, c, bank, gate):
                c0, cn = CHUNKS[c]
                parts = [(0, cn, 0)] if c < 2 else [(0, 256, 0), (256, 320, 1)]
                for j, (a0, a1, m) in enumerate(parts):
                    x = X[:, d, c0 + a0:c0 + a1]
                    ins = V.scalar_tensor_tensor(out=x, in0=ps[bank][:, a0:a1], scalar=MOD[:, gate + d, m:m + 1],
                                                 in1=x, op0=ALU.mult, op1=ALU.add)
                    s.done(ins, name if j == len(parts) - 1 else name + "p")

            dve.sem_inc(w_lo, 1)
            prime(dve, "ffn_dve", "r_dve")
            s = st("in_dve")

            def link(ins, step):
                s.done(ins, step)
                own("in_dve", 0, step)

            wait(dve, "in_act", 0, "ec")
            link(V.tensor_copy(SM[:, 16:36], ps[7][:, 0:20]), "cp")
            link(V.tensor_scalar(SM[:, 0:16], SM[:, 0:16], 1.0, None, ALU.add), "c1")
            link(V.reciprocal(SM[:, 0:16], SM[:, 0:16]), "c2")
            link(V.tensor_tensor(SCV[:].rearrange("p k a -> p a k"), SM[:, 16:32].rearrange("p (a k) -> p a k", a=2),
                                 SM[:, 0:16].rearrange("p (a k) -> p a k", a=2), ALU.mult), "sc")
            lg = SM[:, 32:36]
            link(V.tensor_tensor(SM[:, 40:42], lg[:, 0:2], lg[:, 2:4], ALU.max), "m")
            for i in range(2):
                link(V.tensor_tensor(SM[:, 42 + 2 * i:44 + 2 * i], lg[:, 2 * i:2 * i + 2], SM[:, 40:42], ALU.subtract), f"s{i}")
            wait(dve, "lb_act", 0, "exp")
            link(V.tensor_tensor(SM[:, 46:48], SM[:, 42:44], SM[:, 44:46], ALU.add), "sum")
            link(V.reciprocal(SM[:, 46:48], SM[:, 46:48]), "rsum")
            for i in range(2):
                link(V.tensor_tensor(SM[:, 42 + 2 * i:44 + 2 * i], SM[:, 42 + 2 * i:44 + 2 * i], SM[:, 46:48], ALU.mult), f"p{i}")
            link(V.tensor_tensor(LB[:, 0:2], SM[:, 42:44], SM[:, 42:44], ALU.subtract), "l0")
            link(V.tensor_tensor(LB[:, 2:4], SM[:, 42:44], SM[:, 44:46], ALU.add), "l1")
            link(V.tensor_tensor(LB[:, 2:4], LB[:, 2:4], SM[:, 42:44], ALU.subtract), "lbd")

            with dve.Fori(0, DEPTH) as l:
                s = st("par_dve")
                wait(dve, "par_pe", l, "rows")
                s.done(V.tensor_copy(PRM[:], ps[5][:, 0:65]), "prm")
                s.done(V.tensor_copy(LBL[:, 0:2], LB[:, bass.ds(l * 2, 2)]), "lb")
                own("par_dve", l, "lb")
                s.done(V.tensor_scalar(LBL[:, 2:4], LBL[:, 0:2], -1.0, 1.0, ALU.mult, ALU.add), "olb")
                for m in range(3):
                    split_lo(l, m, m)
                wait(dve, "z_act", l, "kghi")
                s = st("kg_dve")
                s.done(V.tensor_tensor(KGS[:, 1], KGW[:], KGS[:, 0].bitcast(F32), ALU.subtract), "kglo")

                def mod_keep(q):
                    dve.wait_ge(mod_pe, l * NMOD + q + 1)
                    V.tensor_tensor(MOD[:, 2 * q:2 * q + 2, :], ps[6 + q % 2][:, 0:4].rearrange("p (k a) -> p k a", k=2),
                                    PRM[:, 2 * q:2 * q + 2].unsqueeze(2).broadcast_to([P, 2, 2]), ALU.add).then_inc(mod_dve, 1)

                for q in range(8):
                    mod_keep(q)
                dve.wait_ge(mod_dve, l * NMOD + 8)
                norm("n1", l, 8, 48)
                for m in range(3, 6):
                    split_lo(l, m, m)
                for q in range(8, 12):
                    mod_keep(q)
                for j in range(3):
                    split_lo(l, 6 + j, 6 + j)
                for q in range(12, 24):
                    mod_keep(q)

                dve.wait_ge(rc_ld, (l + 1) * 48)
                wait(dve, "rs_pool", l, "zs")

                def recur_dve(kind, g, u, n, loaded):
                    s = st(kind + "_dve")
                    s.body()
                    nm = kind + "_dve"
                    nch = n // CHUNK

                    def step(ins, name, now=False):
                        s.done(ins, name)
                        if now:
                            own(nm, g, name)

                    dve.wait_ge(r_ld[u], loaded)
                    step(V.tensor_scalar(rQQ[:, u, 2, 0:n], rQQ[:, u, 2, 0:n], GLA_SCALE, None, ALU.mult), "qscale")
                    wait(dve, kind + "_act", g, "ehf")
                    t1 = rT1[:, :, 0:n]
                    step(V.tensor_scalar(t1, t1, 1.0, None, ALU.add), "e1", True)
                    step(V.reciprocal(t1, t1), "sig", True)
                    for f in range(2):
                        step(V.tensor_scalar(rT1[:, f, 0:n], rT1[:, f, 0:n], LBL[:, 2 + f:3 + f], LBL[:, f:f + 1],
                                             ALU.mult, ALU.add), f"f{f}")
                    own(nm, g, "f1")
                    step(V.tensor_scalar(rKK[:, u, 0:2, 0:n], t1, -1.0, 1.0, ALU.mult, ALU.add), "k01", True)
                    step(V.tensor_scalar(t1, t1, F_MIN, None, ALU.max), "fmax")
                    wait(dve, kind + "_pe", g, "gate")
                    wait(dve, kind + "_act", g, "abs")
                    step(V.tensor_scalar(rT3[:, 0:n], ps[7][:, 0:n], PRM[:, 64:65], 0.0, ALU.add, ALU.min), "ming", True)
                    wait(dve, kind + "_act", g, "labs")
                    step(V.tensor_tensor(rT3[:, 0:n], rT3[:, 0:n], rT2[:, 0:n], ALU.subtract), "lsg", True)
                    step(V.tensor_scalar(rG[:, 2, 0:n], rT3[:, 0:n], 1.0 / TAU, None, ALU.mult), "g2", True)
                    wait(dve, kind + "_act", g, "lnf")
                    for f in range(3):
                        step(V.tensor_tensor_scan(rB[:, f, 0:n], r_cst[:, R_RM:R_RM + n], rG[:, f, 0:n], 0.0,
                                                  ALU.mult, ALU.add), f"b{f}")
                    own(nm, g, "b2")

                    def dist(lv):
                        b_ = LEVELS[lv - 1]
                        nb = n // (2 * b_)
                        o = rD[:, lv % 2, :, 0:n].rearrange("p f (n c) -> p f n c", c=2 * b_)
                        v = rB[:, :, 0:n].rearrange("p f (n c) -> p f n c", c=2 * b_)
                        if n == P:
                            o = rD[:, lv % 2].rearrange("p f (n c) -> p (f n) c", c=2 * b_)
                            v = rB[:].rearrange("p f (n c) -> p (f n) c", c=2 * b_)
                            r = v[:, :, b_ - 1:b_].broadcast_to([P, 3 * nb, b_])
                            step(V.tensor_tensor(o[:, :, b_:2 * b_], v[:, :, b_:2 * b_], r, ALU.subtract), f"d{lv}r")
                            step(V.tensor_tensor(o[:, :, 0:b_], r, v[:, :, 0:b_], ALU.subtract), f"d{lv}l")
                        else:
                            for f in range(3):
                                r = v[:, f, :, b_ - 1:b_].broadcast_to([P, nb, b_])
                                step(V.tensor_tensor(o[:, f, :, b_:2 * b_], v[:, f, :, b_:2 * b_], r, ALU.subtract), f"d{lv}r{f}")
                                step(V.tensor_tensor(o[:, f, :, 0:b_], r, v[:, f, :, 0:b_], ALU.subtract),
                                     f"d{lv}l{f}" if f < 2 else f"d{lv}l")

                    def probs(lv):
                        wait(dve, kind + "_pe", g, f"s{lv}")
                        for hb in range(2):
                            src = ps[2 * (lv % 2) + hb][0:n].rearrange("p (h t) -> p h t", h=4)[:, :, 0:n]
                            out = rP[0:n, 4 * hb:4 * hb + 4, 0:n]
                            if lv == 0:
                                ins = V.tensor_tensor(out, src, CST[0:n, 0:n].unsqueeze(1).broadcast_to([n, 4, n]), ALU.mult)
                            else:
                                own(nm, g, f"pr{lv - 1}{'ab'[hb]}")
                                m = r_cst[0:n, R_LM + P * (lv - 1):R_LM + P * (lv - 1) + n].bitcast(I32)
                                settle(dve)
                                ins = V.copy_predicated(out, m.unsqueeze(1).broadcast_to([n, 4, n]), src)
                            step(ins, f"pr{lv}{'ab'[hb]}")

                    dist(1)
                    for lv in range(1, 7):
                        if lv < 6:
                            if lv >= 2:
                                wait(dve, kind + "_act", g, f"e{lv - 1}")
                            dist(lv + 1)
                        else:
                            wait(dve, kind + "_act", g, "e5")
                            for c in range(nch):
                                bl = rB[:, :, CHUNK * c + CHUNK - 1:CHUNK * c + CHUNK].broadcast_to([P, 3, CHUNK])
                                step(V.tensor_tensor(rD[:, 1, :, CHUNK * c:CHUNK * c + CHUNK], bl,
                                                     rB[:, :, CHUNK * c:CHUNK * c + CHUNK], ALU.subtract), f"dl{c}")
                        wait(dve, kind + "_act", g, f"e{lv}")
                        if lv >= 3:
                            wait(dve, kind + "_pe", g, f"s{lv - 2}")
                        step(V.tensor_tensor(rKE[:, lv % 2, :, 0:n], rKK[:, u, :, 0:n], rE[:, lv % 2, :, 0:n], ALU.mult), f"ke{lv}")
                        probs(lv - 1)
                    probs(6)
                    wait(dve, kind + "_act", g, "el")
                    wait(dve, kind + "_pe", g, "s6")
                    step(V.tensor_tensor(rKE[:, 0, :, 0:n], rKK[:, u, :, 0:n], rE[:, 0, :, 0:n], ALU.mult), "kl")
                    wait(dve, kind + "_act", g, "eg")
                    step(V.tensor_scalar(rEG[0:n], rEG[0:n], 1.0, None, ALU.add), "g1", True)
                    step(V.reciprocal(rEG[0:n], rEG[0:n]), "grec")
                    for c in range(nch):
                        wait(dve, kind + "_pe", g, f"ds{c}")
                        if c:
                            own(nm, g, f"st{c - 1}c")
                            wait(dve, kind + "_pe", g, "o0")
                        step(V.tensor_tensor(rDS[:], ps[5 + c][:], r_cst[:, R_BM:R_BM + 512], ALU.mult), f"ds{c}", True)
                        wait(dve, kind + "_act", g, "eb")
                        for f, (o0, on) in enumerate(((0, 128), (128, 128), (256, 256))):
                            e = rE[:, 1, f, CHUNK * c + CHUNK - 1:CHUNK * c + CHUNK]
                            step(V.scalar_tensor_tensor(out=rS[:, 1 - c, o0:o0 + on], in0=rS[:, c, o0:o0 + on], scalar=e,
                                                        in1=rDS[:, o0:o0 + on], op0=ALU.mult, op1=ALU.add),
                                 f"st{c}{'abc'[f]}")
                    wait(dve, kind + "_act", g, "osq")
                    o8 = rO[0:n].rearrange("p (h v) -> p h v", h=8)
                    step(V.tensor_reduce(rSS[0:n], o8, AX.X, ALU.add), "oss")
                    wait(dve, kind + "_act", g, "or")
                    step(V.tensor_tensor(rON[0:n].rearrange("p (h v) -> p h v", h=8),
                                         ps[7][0:n].rearrange("p (h v) -> p h v", h=8),
                                         rSS[0:n].unsqueeze(2).broadcast_to([n, 8, DV]), ALU.mult), "on", True)
                    wait(dve, kind + "_pool", g, "gg1")
                    step(V.tensor_tensor(rOUT[0:n, u], rON[0:n], rEG[0:n], ALU.mult), "fin", True)

                settle(dve)
                with dve.Fori(0, 4) as i:
                    for u in range(2):
                        recur_dve("r", l * 8 + 2 * i + u, u, P, (l * [5, 4][u] + i + 1) * 96)
                dve.wait_ge(rs_ld, (l + 1) * 128)
                recur_dve("rt", l, 0, DEC_SEQ, (l * 5 + 5) * 96)

                s = st("a_dve")
                dve.wait_ge(ac_ld, (l + 1) * 80)
                G_CQ, G_CKV, G_Q, G_K, G_O = 0, 256, 512, 512 + QK, 512 + 2 * QK

                def step(ins, name, now=False):
                    s.done(ins, name)
                    if now:
                        own("a_dve", l, name)

                def k_norm(tag, km, n, before):
                    wait(dve, "a_act", l, f"{tag}ksq")
                    step(V.tensor_reduce(AS[0:n, 3:11], QSQ[0:n, 0:512].rearrange("p (h d) -> p h d", h=8), AX.X, ALU.add),
                         f"kss{km}")
                    wait(dve, "a_act", l, f"{tag}kr")
                    before()
                    knope = KM[0:n, :, 0:NOPE]
                    step(V.tensor_tensor(knope, ps[0][0:n].rearrange("p (h d) -> p h d", h=8),
                                         AS[0:n, 3:11].unsqueeze(2).broadcast_to([n, 8, NOPE]), ALU.mult), f"kn{km}", True)
                    step(V.tensor_tensor(knope, knope, GN[0:n, G_K:G_K + NOPE].unsqueeze(1).broadcast_to([n, 8, NOPE]),
                                         ALU.mult), f"{'pkm' if tag[0] == 'p' else 'km'}{km.strip('p')}_g")

                def rope(x, cos, sin, rot, names):
                    x1, x2 = x[:, :, 0:16], x[:, :, 16:32]
                    step(V.tensor_tensor(rot[:, :, 0:16], x2, sin, ALU.mult), names + "_0")
                    step(V.tensor_tensor(rot[:, :, 16:32], x1, sin, ALU.mult), names + "_1", True)
                    step(V.tensor_tensor(x1, x1, cos, ALU.mult), names + "_2a", True)
                    step(V.tensor_tensor(x2, x2, cos, ALU.mult), names + "_2b", True)
                    step(V.tensor_tensor(x1, x1, rot[:, :, 0:16], ALU.subtract), names + "_2c", True)
                    step(V.tensor_tensor(x2, x2, rot[:, :, 16:32], ALU.add), names + "_3", True)

                for t, (t0, n) in enumerate(TILES):
                    if t == NTILE - 1:
                        for j in range(4):
                            k_norm(f"p{j}_", f"p{j}", P,
                                   (lambda: wait(dve, "a_pe", l, f"p{j - 1}_KTb")) if j else
                                   (lambda: wait(dve, "a_pe", l, f"{t - 1}_KTb")))
                    wait(dve, "a_act", l, f"zr{t}")
                    for j, (nm, c0, c1, gat) in enumerate((("cqn", 0, 256, G_CQ), ("kvn", 256, 512, G_CKV),
                                                           ("krn", 512, 544, G_K + NOPE))):
                        step(V.scalar_tensor_tensor(out=ZT[0:n, c0:c1], in0=ZT[0:n, c0:c1], scalar=AS[0:n, j:j + 1],
                                                    in1=GN[0:n, gat:gat + c1 - c0], op0=ALU.mult, op1=ALU.mult),
                             f"{nm}{t}", j == 2)
                    co = CST[0:n, O_COS + 16 * t:O_COS + 16 * t + 16]
                    si = CST[0:n, O_SIN + 16 * t:O_SIN + 16 * t + 16]
                    rope(ZT[0:n, 512:544].unsqueeze(1), co.unsqueeze(1), si.unsqueeze(1), ROT[0:n, 0:1], f"krope{t}")
                    if t == NTILE - 1:
                        before = lambda: wait(dve, "a_pe", l, "p3_KTb")
                    elif t:
                        before = lambda: wait(dve, "a_pe", l, f"{t - 1}_KTb")
                    else:
                        before = lambda: None
                    k_norm(f"{t}_", f"{t}", n, before)
                    wait(dve, "a_act", l, f"qsq{t}_1")
                    q4 = QSQ[0:n].rearrange("p (h d) -> p h d", h=8)
                    step(V.tensor_reduce(AS[0:n, 3:11], q4[:, :, 0:NOPE], AX.X, ALU.add), f"qs{t}a")
                    step(V.tensor_reduce(AS[0:n, 11:19], q4[:, :, NOPE:QK], AX.X, ALU.add), f"qs{t}b")
                    wait(dve, "a_act", l, f"qr{t}")
                    for b in range(2):
                        qp = ps[5 + b][0:n, 0:384].rearrange("p (h d) -> p h d", h=4)
                        for j, (c0, c1) in enumerate(((0, NOPE), (NOPE, QK))):
                            step(V.tensor_tensor(QM[0:n, 4 * b:4 * b + 4, c0:c1], qp[:, :, c0:c1],
                                                 AS[0:n, 3 + 8 * j + 4 * b:7 + 8 * j + 4 * b].unsqueeze(2)
                                                 .broadcast_to([n, 4, c1 - c0]), ALU.mult), f"qn{t}_{b}{j}")
                    own("a_dve", l, f"qn{t}_11")
                    step(V.tensor_tensor(QM[0:n], QM[0:n], GN[0:n, G_Q:G_Q + QK].unsqueeze(1).broadcast_to([n, 8, QK]),
                                         ALU.mult), f"qg{t}", True)
                    rope(QM[0:n, :, NOPE:QK], co.unsqueeze(1).broadcast_to([n, 8, 16]),
                         si.unsqueeze(1).broadcast_to([n, 8, 16]), ROT[0:n], f"qrope{t}")
                    keys = P * (t + 1) if t < 8 else PAST + DEC_SEQ
                    nk = -(-keys // P)

                    def head_max(h):
                        b0 = 2 * (h % 2)
                        wait(dve, "a_pe", l, f"S{t}_{h}")
                        mx = AS[0:n, 50 + 2 * (h % 2):52 + 2 * (h % 2)]
                        parts = [(0, min(512, keys))] + ([(512, keys)] if keys > 512 else [])
                        for j, (k0, k1) in enumerate(parts):
                            step(V.tensor_reduce(mx[:, j:j + 1], ps[b0 + j][0:n, 0:k1 - k0], AX.X, ALU.max), f"mx{t}_{h}{j}", True)
                        if len(parts) == 2:
                            step(V.tensor_tensor(mx[:, 0:1], mx[:, 0:1], mx[:, 1:2], ALU.max), f"mx{t}_{h}m", True)
                        step(V.tensor_scalar(AS[0:n, 24 + h:25 + h], mx[:, 0:1], -MLA_SCALE, None, ALU.mult), f"mx{t}_{h}n")

                    head_max(0)
                    for h in range(HEADS):
                        if h + 1 < HEADS:
                            head_max(h + 1)
                        wait(dve, "a_pe", l, f"T{t}_{h}")
                        if h >= 2:
                            wait(dve, "a_pe", l, f"PV{t}_{h - 2}")
                        for j in range(2 if nk > 4 else 1):
                            kk = min(4, nk - 4 * j)
                            full = kk if (t < 8 or 4 * j + kk < nk) else kk - 1
                            if full:
                                step(V.tensor_copy(PT[:, h % 2, 4 * j:4 * j + full, 0:n],
                                                   ps[4 + j][:, 0:P * full].rearrange("p (k t) -> p k t", k=full)[:, :, 0:n]),
                                     f"pt{t}_{h}_{j}")
                            else:
                                step(V.tensor_copy(PT[0:DEC_SEQ, h % 2, 4 * j, 0:n], ps[4 + j][0:DEC_SEQ, 0:n]), f"pt{t}_{h}_{j}")
                    wait(dve, "a_act", l, f"p{t}_7_{1 if keys > 512 else 0}")
                    sums = AS[0:n, 32:48].rearrange("p (h j) -> p h j", j=2)
                    if keys > 512:
                        step(V.tensor_tensor(sums[:, :, 0], sums[:, :, 0], sums[:, :, 1], ALU.add), f"sm{t}", True)
                    step(V.reciprocal(AS[0:n, 54:62], sums[:, :, 0]), f"rc{t}", True)
                    wait(dve, "a_pe", l, f"PV{t}_7")
                    if t:
                        dve.wait_ge(a_out, (l * NTILE + t) * 16)
                    step(V.tensor_tensor(OM[0:n].rearrange("p (h v) -> p h v", h=8),
                                         ps[7][0:n].rearrange("p (h v) -> p h v", h=8),
                                         AS[0:n, 54:62].unsqueeze(2).broadcast_to([n, 8, VDIM]), ALU.mult), f"on0{t}")
                    wait(dve, "a_act", l, f"or{t}")
                    step(V.scalar_tensor_tensor(out=OM[0:n], in0=OM[0:n], scalar=AS[0:n, 48:49],
                                                in1=GN[0:n, G_O:G_O + 512], op0=ALU.mult, op1=ALU.mult), f"on{t}", True)

                s = st("mix_dve")
                for t, (t0, n) in enumerate(TILES):
                    for b in range(2):
                        wait(dve, "mix_act", l, f"m{t}{'ab'[b]}")
                        src = ps[2 * (t % 2) + b][:].rearrange("p (k t) -> p k t", k=4)[:, :, 0:n]
                        hi = A[:, 0, 4 * b:4 * b + 4, t0:t0 + n].bitcast(F32)
                        s.done(V.tensor_tensor(A[:, 1, 4 * b:4 * b + 4, t0:t0 + n], src, hi, ALU.subtract), f"m{t}{'ab'[b]}")
                for m in range(9, 12):
                    split_lo(l, m, m + 3)
                dve.wait_ge(mod_dve, (l + 1) * NMOD)
                s = st("wo_dve")
                for q in range(24):
                    wait(dve, "wo_pe", l, f"o{q}")
                    residual(s, f"o{q}", q // 3, q % 3, q % 6, 16)
                    if q == 5:
                        split_lo(l, 12, 15)
                    if q in (11, 17, 23):
                        split_lo(l, 13 + (q - 11) // 6, 16 + (q - 11) // 6)
                norm("n2", l, 32, 56)

                def group(g, i, last):
                    s = st("ffn_dve")
                    s.body()
                    for p in range(6):
                        c0, cn = CHUNKS[p % 3]
                        wait(dve, "ffn_act", g, f"sil{p}")
                        wait(dve, "ffn_pe", g, f"u{p}")
                        if p >= 2:
                            own("ffn_dve", g, f"lo{p - 2}")
                        s.done(V.tensor_tensor(HF32[:, p % 2, 0:cn], ps[2 * (p % 3) + 1][:, 0:cn], SIL[:, p % 2, 0:cn],
                                               ALU.mult), f"mul{p}")
                        wait(dve, "ffn_act", g, f"hi{p}")
                        s.done(V.tensor_tensor(HID[:, 1, p // 3, c0:c0 + cn], HF32[:, p % 2, 0:cn],
                                               HID[:, 0, p // 3, c0:c0 + cn].bitcast(F32), ALU.subtract), f"lo{p}")
                    for q in range(24):
                        wait(dve, "ffn_pe", g, f"x{q}")
                        residual(s, f"x{q}", q // 3, q % 3, q % 6, 40)
                        if not last and q in (5, 11, 23):
                            j = (5, 11, 23).index(q)
                            dve.wait_ge(w_hi, hi_val(l, 16 + j) + 3 * i)
                            V.tensor_tensor(W[:, (13 + j) % 3, 1], WR[:, (16 + j) % 3], W[:, (13 + j) % 3, 0].bitcast(F32),
                                            ALU.subtract).then_inc(w_lo, 1)

                settle(dve)
                with dve.Fori(0, NGROUP - 1) as i:
                    group(l * NGROUP + i, i, False)
                group(l * NGROUP + NGROUP - 1, NGROUP - 1, True)

            s = st("out_dve")
            for t, (t0, n) in enumerate(TILES):
                if t >= 2:
                    dve.wait_ge(y_out[t % 2], 16 * (t // 2))
                for b in range(2):
                    wait(dve, "out_pe", 0, f"y{t}{'ab'[b]}")
                    s.done(V.tensor_copy(XT[0:n, t % 2, 512 * b:512 * b + 512], ps[2 * (t % 2) + b][0:n]), f"y{t}{'ab'[b]}")

    return {k: v.seen for k, v in steps.items()}


OUTS = [("y_prompt", (1, SEQ, D_MODEL)), ("y_sample", (1, DEC_SEQ, D_MODEL)),
        ("ckv_p", (DEPTH, 1, SEQ, RANK)), ("kr_p", (DEPTH, 1, SEQ, ROPE)),
        ("hg_p", (DEPTH, 1, HG_H, HG_DK, DV)), ("gla_p", (DEPTH, 1, GLA_H, GLA_DK, DV)),
        ("ckv_s", (DEPTH, 1, DEC_SEQ, RANK)), ("kr_s", (DEPTH, 1, DEC_SEQ, ROPE)),
        ("hg_s", (DEPTH, 1, HG_H, HG_DK, DV)), ("gla_s", (DEPTH, 1, GLA_H, GLA_DK, DV))]


def kernel(**inputs):
    import numpy as _np
    import concourse.bacc as _bacc
    from concourse.bass_utils import run_bass_kernel_spmd as _run

    arrays = {k: _np.ascontiguousarray(v) for k, v in inputs.items()}
    arrays["cst"], arrays["cst_r"] = constants()
    plan = {}
    for _ in range(2):
        nc = _bacc.Bacc("TRN2", target_bir_lowering=False, num_devices=1)
        nc.disable_value_cache = True
        io = {}
        for name, a in arrays.items():
            io[name] = nc.dram_tensor("in_" + name, list(a.shape), F32, kind="ExternalInput").ap()
        for name, shape in OUTS:
            io[name] = nc.dram_tensor("out_" + name, list(shape), F32, kind="ExternalOutput").ap()
        plan = program(nc, io, plan)
    r = _run(nc, [{"in_" + k: v for k, v in arrays.items()}], core_ids=[0])
    return tuple(r.results[0]["out_" + n] for n, _ in OUTS)
```
